# Optimizing a Trainium2 kernel written in Bass

```python
import math
import jax, jax.numpy as jnp
from jax import lax
import numpy as np

D_MODEL = 1024
BATCH = 1
SEQ = 2048
DEPTH = 1

CHUNK = 64
Q_BLOCK = 128
MIX_WIDTH = D_MODEL
DIFF_WIDTH = MIX_WIDTH // 2
HGRN_WIDTH = MIX_WIDTH - DIFF_WIDTH
DIFF_HEAD_DIM = 64
DIFF_HEADS = DIFF_WIDTH // (2 * DIFF_HEAD_DIM)
HGRN_EXPAND = 128
HGRN_HEADS = HGRN_WIDTH // HGRN_EXPAND
HGRN_DK = HGRN_EXPAND
HGRN_DV = HGRN_WIDTH // HGRN_HEADS
D_FF = ((8 * D_MODEL + 3 * 256 - 1) // (3 * 256)) * 256
NORM_EPS = 1e-6

IN_WIDTHS = (
    2 * DIFF_HEADS * DIFF_HEAD_DIM,
    2 * DIFF_HEADS * DIFF_HEAD_DIM,
    DIFF_HEADS * 2 * DIFF_HEAD_DIM,
    HGRN_HEADS * HGRN_DK,
    HGRN_HEADS * HGRN_DK,
    HGRN_HEADS * HGRN_DV,
    HGRN_HEADS * HGRN_DV,
)
D_IN = sum(IN_WIDTHS)
SPLIT_POINTS = tuple(int(v) for v in np.cumsum(IN_WIDTHS)[:-1])

kernel_name = "hymba_diffattn_hgrn2_trunk"

def rms_norm(x, g):
    xf = x.astype(jnp.float32)
    y = xf * lax.rsqrt(jnp.mean(xf * xf, axis=-1, keepdims=True) + NORM_EPS)
    return (y * g.astype(jnp.float32)).astype(x.dtype)

def diff_attention(q, k, v, lam):
    B, H2, S, Dh = q.shape
    H = H2 // 2
    nb = S // Q_BLOCK
    qb = q.reshape(B, H2, nb, Q_BLOCK, Dh).transpose(2, 0, 1, 3, 4)
    key_chunk = jnp.arange(S) // CHUNK

    def one_block(args):
        q_blk, blk = args
        q_chunk = (blk * Q_BLOCK + jnp.arange(Q_BLOCK)) // CHUNK
        mask = key_chunk[None, :] <= q_chunk[:, None]
        s = jnp.einsum('bhqd,bhkd->bhqk', q_blk, k).astype(jnp.float32)
        p = jax.nn.softmax(jnp.where(mask, s, -jnp.inf), axis=-1)
        p = p.reshape(B, H, 2, Q_BLOCK, S)
        w = p[:, :, 0] - lam * p[:, :, 1]
        return jnp.einsum('bhqk,bhkv->bhqv', w.astype(v.dtype), v)

    out = lax.map(one_block, (qb, jnp.arange(nb)))
    return out.transpose(1, 2, 0, 3, 4).reshape(B, H, S, v.shape[-1])

def hgrn2_chunked(q, k, v, lf):
    B, S, H, dk = q.shape
    dv = v.shape[-1]
    nc = S // CHUNK

    def to_chunks(t):
        return t.reshape(B, nc, CHUNK, H, t.shape[-1]).transpose(1, 0, 3, 2, 4)

    qc, kc, vc, lfc = to_chunks(q), to_chunks(k), to_chunks(v), to_chunks(lf)
    bc = jnp.cumsum(lfc, axis=3)
    causal = jnp.tril(jnp.ones((CHUNK, CHUNK), dtype=bool))

    def step(state, inp):
        q_c, k_c, v_c, b_c = inp
        diff = b_c[:, :, :, None, :] - b_c[:, :, None, :, :]
        decay = jnp.exp(jnp.where(causal[:, :, None], diff, -jnp.inf))
        scores = jnp.einsum('bhtk,bhsk,bhtsk->bhts', q_c, k_c, decay)
        o = (jnp.einsum('bhts,bhsv->bhtv', scores, v_c)
             + jnp.einsum('bhtk,bhkv->bhtv', q_c * jnp.exp(b_c), state))
        b_last = b_c[:, :, -1:, :]
        state = (jnp.exp(b_last[:, :, 0, :, None]) * state
                 + jnp.einsum('bhsk,bhsv->bhkv', k_c * jnp.exp(b_last - b_c), v_c))
        return state, o

    state0 = jnp.zeros((B, H, dk, dv), jnp.float32)
    _, o = lax.scan(step, state0, (qc, kc, vc, bc))
    return o.transpose(1, 0, 3, 2, 4).reshape(B, S, H, dv)

def setup_inputs(seed: int = 0) -> dict:
    key = jax.random.key(seed)
    ks = jax.random.split(key, 17)

    def normal(k, shape, scale):
        return jax.random.normal(k, shape, jnp.float32) * scale

    return {
        "x": normal(ks[0], (BATCH, SEQ, D_MODEL), 1.0),
        "attn_norm_g": 1.0 + normal(ks[1], (DEPTH, D_MODEL), 0.02),
        "w_in": normal(ks[2], (DEPTH, D_MODEL, D_IN), D_MODEL ** -0.5),
        "q_norm_g": 1.0 + normal(ks[3], (DEPTH, DIFF_HEAD_DIM), 0.02),
        "k_norm_g": 1.0 + normal(ks[4], (DEPTH, DIFF_HEAD_DIM), 0.02),
        "lambda_q1": normal(ks[5], (DEPTH, DIFF_HEAD_DIM), 0.1),
        "lambda_k1": normal(ks[6], (DEPTH, DIFF_HEAD_DIM), 0.1),
        "lambda_q2": normal(ks[7], (DEPTH, DIFF_HEAD_DIM), 0.1),
        "lambda_k2": normal(ks[8], (DEPTH, DIFF_HEAD_DIM), 0.1),
        "subln_g": 1.0 + normal(ks[9], (DEPTH, 2 * DIFF_HEAD_DIM), 0.02),
        "lower_bounds": normal(ks[10], (DEPTH, HGRN_HEADS * HGRN_DK), 0.1),
        "hgrn_norm_g": 1.0 + normal(ks[11], (DEPTH, HGRN_DV), 0.02),
        "w_out": normal(ks[12], (DEPTH, MIX_WIDTH, D_MODEL), MIX_WIDTH ** -0.5),
        "ffn_norm_g": 1.0 + normal(ks[13], (DEPTH, D_MODEL), 0.02),
        "w_gate": normal(ks[14], (DEPTH, D_MODEL, D_FF), D_MODEL ** -0.5),
        "w_up": normal(ks[15], (DEPTH, D_MODEL, D_FF), D_MODEL ** -0.5),
        "w_down": normal(ks[16], (DEPTH, D_FF, D_MODEL), D_FF ** -0.5),
    }

def reference(x, attn_norm_g, w_in, q_norm_g, k_norm_g, lambda_q1, lambda_k1,
              lambda_q2, lambda_k2, subln_g, lower_bounds, hgrn_norm_g, w_out,
              ffn_norm_g, w_gate, w_up, w_down):
    B, S, _ = x.shape
    gamma = jax.nn.softmax(lower_bounds.astype(jnp.float32), axis=0)
    lbs = jnp.cumsum(gamma, axis=0) - gamma[0]

    for l in range(DEPTH):
        h = rms_norm(x, attn_norm_g[l])
        proj = jnp.einsum('bsd,de->bse', h, w_in[l])
        qd, kd, vd, qr, fr, ir, gr = jnp.split(proj, SPLIT_POINTS, axis=-1)

        qd = rms_norm(qd.reshape(B, S, 2 * DIFF_HEADS, DIFF_HEAD_DIM), q_norm_g[l]) * (DIFF_HEAD_DIM ** -0.5)
        kd = rms_norm(kd.reshape(B, S, 2 * DIFF_HEADS, DIFF_HEAD_DIM), k_norm_g[l])
        vd = vd.reshape(B, S, DIFF_HEADS, 2 * DIFF_HEAD_DIM)
        lam_init = 0.8 - 0.6 * math.exp(-0.3 * l)
        lam = (jnp.exp(jnp.sum(lambda_q1[l].astype(jnp.float32) * lambda_k1[l].astype(jnp.float32)))
               - jnp.exp(jnp.sum(lambda_q2[l].astype(jnp.float32) * lambda_k2[l].astype(jnp.float32)))
               + lam_init)
        od = diff_attention(qd.transpose(0, 2, 1, 3), kd.transpose(0, 2, 1, 3),
                            vd.transpose(0, 2, 1, 3), lam)
        od = rms_norm(od, subln_g[l]) * (1.0 - lam_init)
        od = od.transpose(0, 2, 1, 3).reshape(B, S, DIFF_WIDTH)

        fz = fr.astype(jnp.float32).reshape(B, S, HGRN_HEADS, HGRN_DK)
        if l == 0:
            lf = jax.nn.log_sigmoid(fz)
        else:
            lb = lbs[l].reshape(HGRN_HEADS, HGRN_DK)
            lf = jnp.log(lb + (1.0 - lb) * jax.nn.sigmoid(fz))
        kr = -jnp.expm1(lf)
        qr = jax.nn.silu(qr.astype(jnp.float32)).reshape(B, S, HGRN_HEADS, HGRN_DK)
        vr = ir.astype(jnp.float32).reshape(B, S, HGRN_HEADS, HGRN_DV)
        orr = hgrn2_chunked(qr, kr, vr, lf).astype(x.dtype)
        orr = rms_norm(orr, hgrn_norm_g[l]) * jax.nn.silu(gr.reshape(B, S, HGRN_HEADS, HGRN_DV))
        orr = orr.reshape(B, S, HGRN_WIDTH)

        mix = jnp.concatenate([od.astype(x.dtype), orr.astype(x.dtype)], axis=-1)
        x = x + jnp.einsum('bse,ed->bsd', mix, w_out[l])

        h = rms_norm(x, ffn_norm_g[l])
        ff = jax.nn.silu(jnp.einsum('bsd,df->bsf', h, w_gate[l])) * jnp.einsum('bsd,df->bsf', h, w_up[l])
        x = x + jnp.einsum('bsf,fd->bsd', ff, w_down[l])
    return x


_drawn_inputs = setup_inputs


def setup_inputs(seed=0):
    import zlib

    import numpy as np

    out = dict(_drawn_inputs(seed))
    spreads = {}
    factors = {'q_norm_g': 4.432,
     'k_norm_g': 5.52,
     'lambda_q1': 8.0,
     'lambda_k2': 2.952,
     'subln_g': 4.934,
     'hgrn_norm_g': 6.869,
     'ffn_norm_g': 4.325}
    for name, (base, spread) in spreads.items():
        noise = np.random.default_rng([zlib.crc32(name.encode()), seed]).standard_normal(out[name].shape)
        drawn = base * np.exp(spread * noise) if base else spread * noise
        out[name] = __import__('jax').numpy.asarray(drawn.astype(out[name].dtype))
    for name, factor in factors.items():
        out[name] = (out[name] * factor).astype(out[name].dtype)
    return out
```

```python
from contextlib import ExitStack

import concourse.bass as bass
from concourse import mybir

P = 128
D = 1024
SEQ = 2048
DH = 64
HEADS = 4
W = 512
D_FF = 2816
EPS = 1e-6
LAM_INIT = 0.8 - 0.6

TB = 512
BLOCKS = SEQ // TB
SUB = TB // P
KS = D // P
UC = 256
UT = UC // P

F32 = mybir.dt.float32
F32R = mybir.dt.float32r

ALU = mybir.AluOpType
ACT = mybir.ActivationFunctionType
AX = mybir.AxisListType


class Count:

    def __init__(self, sem, credit=0):
        self.sem, self.credit = sem, credit

    def wait(self, eng, value):
        eng.wait_ge(self.sem, value + self.credit)


class Alloc:

    def __init__(self, nc, ctx, prefix):
        self.nc, self.ctx, self.prefix = nc, ctx, prefix

    def sb(self, name, shape, dt=F32):
        return self.ctx.enter_context(self.nc.sbuf_tensor(f"{self.prefix}_{name}", shape, dt))

    def bank(self, name):
        return self.ctx.enter_context(self.nc.psum_tensor(f"{self.prefix}_{name}", [P, 512], F32))

    def sem(self, name):
        return self.ctx.enter_context(self.nc.semaphore(f"{self.prefix}_{name}"))


def make_constants(nc, ident, pair_sel, ones, eps):
    with ExitStack() as ctx:
        a = Alloc(nc, ctx, "const")
        ident_zeroed = a.sem("ident_zeroed")
        pair_zeroed = a.sem("pair_zeroed")
        block = ctx.enter_context(nc.Block())

        @block.gpsimd
        def _(pool):
            nc.gpsimd.memset(ident[:], 0.0).then_inc(ident_zeroed, 1)
            pool.wait_ge(ident_zeroed, 1)
            nc.gpsimd.affine_select(out=ident[:], in_=ident[:], compare_op=ALU.not_equal, fill=1.0, base=0,
                                    pattern=[[-1, P]], channel_multiplier=1)

        @block.vector
        def _(dve):
            nc.vector.memset(pair_sel[:], 0.0).then_inc(pair_zeroed, 1)
            nc.vector.memset(ones[:], 1.0)
            nc.vector.memset(eps[:], EPS)
            dve.wait_ge(pair_zeroed, 1)
            for m in range(2):
                part = slice(m * DH, (m + 1) * DH)
                nc.vector.memset(pair_sel[part, m:m + 1], 1.0)


def project(nc, x, attn_g, w_in, q_g, k_g, ident, pair_sel, eps, out):
    UNITS = w_in.shape[1] // UC
    PER_TURN = 2 * UNITS
    QK, V, HQ, HF, HI, HG = range(4), range(4, 6), range(6, 8), range(8, 10), range(10, 12), range(12, 14)
    TOKEN_MAJOR = (*V, *HI, *HG)
    SQUARES = {4: (0, 1), 5: (2, 3)}
    SCALE_STEP = 6
    SLABS = {7: (0, 1), 8: (2,), 9: (3,), 10: (4,), 11: (5,), 12: (6,), 13: (7,)}
    w_view = w_in.rearrange("(s p) n -> p s n", p=P)

    with ExitStack() as ctx:
        a = Alloc(nc, ctx, "proj")
        x_tok = a.sb("x_tok", [P, SUB, D])
        junk = a.sb("junk", [P, D])
        x_sumsq = a.sb("x_sumsq", [P, SUB])
        x_rms = a.sb("x_rms", [P, SUB])
        x_rrms = a.sb("x_rrms", [P, SUB])
        g_col = a.sb("g_col", [P, KS])
        qk_g = a.sb("qk_g", [P, 2])
        qk_gs = a.sb("qk_gs", [P, 2])
        h_hi = [a.sb(f"h_hi{b}", [P, KS, TB], F32R) for b in range(2)]
        h_lo = [a.sb(f"h_lo{b}", [P, KS, TB], F32R) for b in range(2)]
        w_raw = [a.sb(f"w_raw{b}", [P, KS, UC]) for b in range(2)]
        w_hi = [a.sb(f"w_hi{b}", [P, KS, UC], F32R) for b in range(2)]
        w_lo = [a.sb(f"w_lo{b}", [P, KS, UC], F32R) for b in range(2)]
        qk_raw = a.sb("qk_raw", [P, UT, TB])
        qk_sq = a.sb("qk_sq", [P, UT, TB])
        qk_rms = a.sb("qk_rms", [P, UT, SUB * 2])
        qk_rrms = a.sb("qk_rrms", [P, UT, SUB * 2])
        qk_spread = a.sb("qk_spread", [P, UT, SUB, P])
        stage = [[a.sb(f"stage{b}{k}", [P, UT, TB]) for k in range(2)] for b in range(2)]
        prod = [[a.bank(f"prod{b}{t}") for t in range(UT)] for b in range(2)]
        turned = [a.bank(f"turned{b}") for b in range(2)]
        sums = [a.bank(f"sums{t}") for t in range(UT)]

        waited = a.sem("waited")
        gains_in = a.sem("gains_in")
        gain_scaled = a.sem("gain_scaled")
        x_in = a.sem("x_in")
        w_in_sem = [a.sem(f"w_in{b}") for b in range(2)]
        w_hi_made = a.sem("w_hi_made")
        w_lo_made = a.sem("w_lo_made")
        unit_done = Count(a.sem("unit_done"), 1)
        squares_made = a.sem("squares_made")
        x_rms_made = a.sem("x_rms_made")
        x_rrms_made = a.sem("x_rrms_made")
        x_scaled = a.sem("x_scaled")
        slab_turned = a.sem("slab_turned")
        h_hi_made = a.sem("h_hi_made")
        h_lo_made = a.sem("h_lo_made")
        raw_made = a.sem("raw_made")
        sq_made = a.sem("sq_made")
        sums_made = a.sem("sums_made")
        rms_made = a.sem("rms_made")
        rrms_made = a.sem("rrms_made")
        widened = a.sem("widened")
        spread = a.sem("spread")
        norm_made = a.sem("norm_made")
        norm_hi_made = a.sem("norm_hi_made")
        act_part = a.sem("act_part")
        finished = [Count(a.sem(f"finished{b}"), 1) for b in range(2)]
        stored = [Count(a.sem(f"stored{b}"), 16) for b in range(2)]
        block = ctx.enter_context(nc.Block())

        def tokens_after(i, p):
            return (2 * i + 1) * TB if p == 0 else (1 - i) * 2 * TB

        def feature_dst(array, u0, u, tok):
            return array[(u - u0) * UC:(u - u0 + 1) * UC, bass.ds(tok, TB)].rearrange("(t p) n -> p t n", p=P)

        def token_dst(array, u0, u, tok):
            return array[bass.ds(tok, TB), (u - u0) * UC:(u - u0 + 1) * UC].rearrange("(t p) n -> p t n", p=P)

        def destinations(u, tok):
            if u in QK:
                return [feature_dst(out[k], 0, u, tok) for k in ("qk_hi", "qk_lo")]
            if u in V:
                return [token_dst(out[k], V[0], u, tok) for k in ("v_hi", "v_lo")]
            if u in HQ:
                return [feature_dst(out["hq"], HQ[0], u, tok)]
            if u in HF:
                return [feature_dst(out[k], HF[0], u, tok) for k in ("hf", "hk")]
            return [token_dst(out["hv"], HI[0], u, tok) if u in HI else token_dst(out["hgate"], HG[0], u, tok)]

        def stored_before(par, n):
            return sum(16 * len(destinations(m % UNITS, 0)) for m in range(n) if m % 2 == par)

        STORED_PER_TURN = [stored_before(par, PER_TURN) for par in range(2)]

        def staged_view(u, k, par):
            t = stage[par][k][:]
            if u in TOKEN_MAJOR:
                return t.rearrange("p t (b n) -> p (t b) n", b=2)
            return t

        @block.sync
        def _(sp):
            sp.dma_start(g_col[:], attn_g.rearrange("(s p) -> p s", p=P), allow_slow_non_contiguous=True).then_inc(gains_in, 16)
            for m in range(2):
                part = slice(m * DH, (m + 1) * DH)
                sp.dma_start(qk_g[part, 0:1], q_g.rearrange("(p o) -> p o", o=1)).then_inc(gains_in, 16)
                sp.dma_start(qk_g[part, 1:2], k_g.rearrange("(p o) -> p o", o=1)).then_inc(gains_in, 16)

            def load_x(tok):
                sp.dma_start(x_tok[:], x[bass.ds(tok, TB), :].rearrange("(t p) d -> p t d", p=P)).then_inc(x_in, 16)

            def load_w(u):
                u = u % UNITS
                sp.dma_start(w_raw[u % 2][:], w_view[:, :, u * UC:(u + 1) * UC]).then_inc(w_in_sem[u % 2], 16)

            def store(i, n):
                u = n % UNITS
                finished[u % 2].wait(sp, i * UNITS + n // 2 + 1)
                sp.sem_inc(waited, 1)
                for k, dst in enumerate(destinations(u, (2 * i + n // UNITS) * TB)):
                    sp.dma_start(dst, staged_view(u, k, u % 2)).then_inc(stored[u % 2].sem, 16)

            load_x(0)
            load_w(0)
            load_w(1)
            with sp.Fori(0, BLOCKS // 2) as i:
                for n in range(PER_TURN):
                    p, u = divmod(n, UNITS)
                    sp.wait_ge(w_lo_made, i * PER_TURN + n + 1)
                    load_w(n + 2)
                    if u == 1:
                        sp.wait_ge(slab_turned, (2 * i + p + 1) * KS)
                        sp.sem_inc(waited, 1)
                        load_x(tokens_after(i, p))
                    store(i, n)
            for par in range(2):
                stored[par].wait(sp, 2 * STORED_PER_TURN[par])
                sp.wait_ge(w_in_sem[par], 16 * (PER_TURN + 1))
            sp.wait_ge(x_in, 16 * (BLOCKS + 1))

        def earlier(par, i, n):
            return i * UNITS + (n + 1 - par) // 2

        HANDED = [(u, t) for u in (*V, *HQ, *HG) for t in range(UT)]

        def handed(i, n, t):
            p, u = divmod(n, UNITS)
            return (2 * i + p) * len(HANDED) + HANDED.index((u, t)) + 1

        @block.scalar
        def _(act):
            def split_w(i, n):
                par = n % 2
                act.wait_ge(w_in_sem[par], i * (16 * UNITS) + 16 * (n // 2 + 1))
                unit_done.wait(act, i * PER_TURN + (n - 1 if n else 0))
                nc.scalar.activation(w_hi[par][:], w_raw[par][:], ACT.Copy).then_inc(w_hi_made, 1)

            def square_x(nb, t):
                if t == 0:
                    act.wait_ge(x_in, (nb + 1) * 16)
                else:
                    act.wait_ge(squares_made, nb * SUB + t)
                nc.scalar.activation(junk[:], x_tok[:, t, :], ACT.Square, accum_out=x_sumsq[:, t:t + 1]).then_inc(squares_made, 1)
                if t == SUB - 1:
                    act.wait_ge(squares_made, (nb + 1) * SUB)
                    nc.scalar.activation(x_rms[:], x_sumsq[:], ACT.Sqrt, bias=eps[:], scale=1.0 / D).then_inc(x_rms_made, 1)

            def h_high(nb, s, buf):
                act.wait_ge(slab_turned, nb * KS + s + 1)
                nc.scalar.activation(h_hi[buf][:, s, :], turned[s % 2][:], ACT.Copy, scale=g_col[:, s:s + 1]).then_inc(h_hi_made, 1)

            def finish(i, n):
                p, u = divmod(n, UNITS)
                par = n % 2
                banks, (first, second) = prod[par], stage[par]
                unit_done.wait(act, i * PER_TURN + n + 1)
                if u in QK:
                    T = (2 * i + p) * (len(QK) * UT) + u * UT
                    finished[1 - par].wait(act, earlier(1 - par, i, n))
                    for t in range(UT):
                        nc.scalar.activation(qk_raw[:, t, :], banks[t][:], ACT.Copy).then_inc(raw_made, 1)
                    for t in range(UT):
                        act.wait_ge(raw_made, T + t + 1)
                        nc.scalar.activation(qk_sq[:, t, :], qk_raw[:, t, :], ACT.Square).then_inc(sq_made, 1)
                    for t in range(UT):
                        act.wait_ge(sums_made, T + t + 1)
                        nc.scalar.activation(qk_rms[:, t, :], sums[t][:, 0:SUB * 2], ACT.Sqrt, bias=eps[:], scale=1.0 / DH).then_inc(rms_made, 1)
                    return
                stored[par].wait(act, i * STORED_PER_TURN[par] + stored_before(par, n))
                for t in range(UT):
                    if u in V:
                        nc.scalar.activation(first[:, t, :].bitcast(F32R), banks[t][:], ACT.Copy).then_inc(act_part, 1)
                    elif u in HQ or u in HG:
                        nc.scalar.activation(second[:, t, :], banks[t][:], ACT.Sigmoid).then_inc(act_part, 1)
                    elif u in HI:
                        last = nc.scalar.activation(first[:, t, :], banks[t][:], ACT.Copy)
                    else:
                        nc.scalar.activation(first[:, t, :], banks[t][:], ACT.Sigmoid)
                        last = nc.scalar.activation(second[:, t, :], banks[t][:], ACT.Sigmoid, scale=-1.0)
                if u in HI or u in HF:
                    last.then_inc(finished[par].sem, 1)

            act.wait_ge(gains_in, 80)
            for t in range(SUB):
                square_x(0, t)
            for s in range(KS):
                h_high(0, s, 0)
            split_w(0, 0)
            with act.Fori(0, BLOCKS // 2) as i:
                for n in range(PER_TURN):
                    p, u = divmod(n, UNITS)
                    nb = 2 * i + p + 1
                    split_w(i, n + 1)
                    for t in SQUARES.get(u, ()):
                        square_x(nb, t)
                    for s in SLABS.get(u, ()):
                        h_high(nb, s, 1 - p)
                    finish(i, n)

        @block.vector
        def _(dve):
            def split_w(i, n):
                par = n % 2
                dve.wait_ge(w_hi_made, i * PER_TURN + n + 1)
                nc.vector.tensor_tensor(w_lo[par][:], w_raw[par][:], w_hi[par][:].bitcast(F32), ALU.subtract).then_inc(w_lo_made, 1)

            def scale_x(nb):
                dve.wait_ge(x_rms_made, nb + 1)
                nc.vector.reciprocal(x_rrms[:], x_rms[:]).then_inc(x_rrms_made, 1)
                dve.wait_ge(x_rrms_made, nb + 1)
                for t in range(SUB):
                    nc.vector.tensor_scalar(x_tok[:, t, :], x_tok[:, t, :], x_rrms[:, t:t + 1], None, ALU.mult).then_inc(x_scaled, 1)

            def h_low(nb, s, buf):
                dve.wait_ge(h_hi_made, nb * KS + s + 1)
                nc.vector.scalar_tensor_tensor(out=h_lo[buf][:, s, :], in0=turned[s % 2][:], scalar=g_col[:, s:s + 1],
                                               in1=h_hi[buf][:, s, :].bitcast(F32), op0=ALU.mult,
                                               op1=ALU.subtract).then_inc(h_lo_made, 1)

            def finish(i, n):
                p, u = divmod(n, UNITS)
                par = n % 2
                banks, (first, second) = prod[par], stage[par]
                if u in QK:
                    T = (2 * i + p) * (len(QK) * UT) + u * UT
                    gain = (qk_gs[:, 0:1], qk_gs[:, 1:2])[u * UC // W]
                    stored[par].wait(dve, i * STORED_PER_TURN[par] + stored_before(par, n))
                    for t in range(UT):
                        dve.wait_ge(rms_made, T + t + 1)
                        nc.vector.reciprocal(qk_rrms[:, t, :], qk_rms[:, t, :]).then_inc(rrms_made, 1)
                        dve.wait_ge(rrms_made, T + t + 1)
                        wide = qk_spread[:, t].rearrange("p b (m f) -> p (b m) f", m=2)
                        nc.vector.tensor_copy(wide, qk_rrms[:, t, :].unsqueeze(2).to_broadcast([P, SUB * 2, DH])).then_inc(widened, 1)
                    for t in range(UT):
                        dve.wait_ge(spread, T + t + 1)
                        nc.vector.scalar_tensor_tensor(out=qk_raw[:, t, :], in0=qk_raw[:, t, :], scalar=gain,
                                                       in1=banks[t][:], op0=ALU.mult, op1=ALU.mult).then_inc(norm_made, 1)
                        dve.wait_ge(norm_made, T + t + 1)
                        nc.vector.tensor_copy(first[:, t, :].bitcast(F32R), qk_raw[:, t, :]).then_inc(norm_hi_made, 1)
                        dve.wait_ge(norm_hi_made, T + t + 1)
                        last = nc.vector.tensor_tensor(second[:, t, :].bitcast(F32R), qk_raw[:, t, :], first[:, t, :], ALU.subtract)
                elif u in V:
                    for t in range(UT):
                        dve.wait_ge(act_part, handed(i, n, t))
                        last = nc.vector.tensor_tensor(second[:, t, :].bitcast(F32R), banks[t][:], first[:, t, :], ALU.subtract)
                elif u in HQ or u in HG:
                    for t in range(UT):
                        dve.wait_ge(act_part, handed(i, n, t))
                        last = nc.vector.tensor_tensor(first[:, t, :], banks[t][:], second[:, t, :], ALU.mult)
                else:
                    return
                last.then_inc(finished[par].sem, 1)

            for count in (unit_done, *finished, *stored):
                dve.sem_inc(count.sem, count.credit)
            dve.wait_ge(gains_in, 80)
            nc.vector.tensor_scalar(qk_gs[:, 0:1], qk_g[:, 0:1], DH ** -0.5, None, ALU.mult).then_inc(gain_scaled, 1)
            nc.vector.tensor_copy(qk_gs[:, 1:2], qk_g[:, 1:2]).then_inc(gain_scaled, 1)
            dve.wait_ge(gain_scaled, 2)
            scale_x(0)
            for s in range(KS):
                h_low(0, s, 0)
            split_w(0, 0)
            with dve.Fori(0, BLOCKS // 2) as i:
                for n in range(PER_TURN):
                    p, u = divmod(n, UNITS)
                    nb = 2 * i + p + 1
                    split_w(i, n + 1)
                    if u == SCALE_STEP:
                        scale_x(nb)
                    for s in SLABS.get(u, ()):
                        h_low(nb, s, 1 - p)
                    finish(i, n)

        @block.tensor
        def _(pe):
            def turn_slab(nb, s, first_block=False):
                pe.wait_ge(x_scaled, (nb + 1) * SUB)
                if not (first_block and s < 2):
                    pe.wait_ge(h_lo_made, nb * KS + s - 1)
                for t in range(SUB):
                    last = pe.transpose(turned[s % 2][:, t * P:(t + 1) * P], x_tok[:, t, s * P:(s + 1) * P], ident[:])
                last.then_inc(slab_turned, 1)

            def sum_squares(i, n):
                p, u = divmod(n, UNITS)
                T = (2 * i + p) * (len(QK) * UT) + u * UT
                for t in range(UT):
                    pe.wait_ge(sq_made, T + t + 1)
                    for b in range(SUB):
                        last = pe.matmul(sums[t][:, 2 * b:2 * b + 2], qk_sq[:, t, b * P:(b + 1) * P], pair_sel[:],
                                         start=True, stop=True)
                    last.then_inc(sums_made, 1)

            def spread_scales(i, n):
                p, u = divmod(n, UNITS)
                T = (2 * i + p) * (len(QK) * UT) + u * UT
                for t in range(UT):
                    pe.wait_ge(widened, T + t + 1)
                    for b in range(SUB):
                        last = pe.matmul(prod[n % 2][t][:, b * P:(b + 1) * P], qk_spread[:, t, b, :], ident[:],
                                         start=True, stop=True)
                    last.then_inc(spread, 1)

            for s in range(KS):
                turn_slab(0, s, True)
            pe.wait_ge(h_lo_made, KS)
            with pe.Fori(0, BLOCKS // 2) as i:
                for n in range(PER_TURN):
                    p, u = divmod(n, UNITS)
                    par = n % 2
                    nb = 2 * i + p + 1
                    hi, lo, wh, wl = h_hi[p], h_lo[p], w_hi[par], w_lo[par]
                    if u == 0:
                        pe.wait_ge(h_lo_made, nb * KS)
                    pe.wait_ge(w_lo_made, i * PER_TURN + n + 1)
                    finished[par].wait(pe, i * UNITS + n // 2)

                    def other_work(quarter):
                        if u and u - 1 in QK:
                            if quarter == 1:
                                sum_squares(i, n - 1)
                            elif quarter == 2:
                                spread_scales(i, n - 1)
                        elif quarter == 1:
                            for s in SLABS.get(u, ()):
                                turn_slab(nb, s)

                    if u in TOKEN_MAJOR:
                        for t in range(SUB):
                            dst = prod[par][t // 2][:, (t % 2) * UC:(t % 2 + 1) * UC]
                            tok = slice(t * P, (t + 1) * P)
                            for s in range(KS):
                                pe.matmul(dst, hi[:, s, tok], wh[:, s, :], start=s == 0, stop=False)
                                pe.matmul(dst, hi[:, s, tok], wl[:, s, :], start=False, stop=False)
                                last = pe.matmul(dst, lo[:, s, tok], wh[:, s, :], start=False, stop=s == KS - 1)
                            if t < 2:
                                other_work(t + 1)
                    else:
                        for t in range(UT):
                            dst = prod[par][t][:]
                            col = slice(t * P, (t + 1) * P)
                            for s in range(KS):
                                pe.matmul(dst, wh[:, s, col], hi[:, s, :], start=s == 0, stop=False)
                                pe.matmul(dst, wh[:, s, col], lo[:, s, :], start=False, stop=False)
                                last = pe.matmul(dst, wl[:, s, col], hi[:, s, :], start=False, stop=s == KS - 1)
                                if t == 0 and s % (KS // 2) == KS // 2 - 1:
                                    other_work(1 + s // (KS // 2))
                    last.then_inc(unit_done.sem, 1)


def attend(nc, mid, lambdas, subln_g, ident, eps, mix):
    STEPS = SEQ // P
    RING = 5
    GROUP = 512 // P
    MASKED = -1e30

    def banks_of(j):
        return j // GROUP + 1

    runs, at = {}, 0
    for j in range(STEPS):
        for m in range(2):
            runs[j, m], key, left = [], 0, (j + 1) * P
            while left:
                n = min(RING - at, -(-left // 512))
                width = min(left, n * 512)
                runs[j, m].append((at, key, width))
                at, key, left = (at + n) % RING, key + width, left - width
    assert at == 0
    order = [(j, m, r) for j in range(STEPS) for m in range(2) for r in range(len(runs[j, m]))]
    RUNS = len(order)
    RUN_AT = {key: n for n, key in enumerate(order)}
    freed, last_in = {}, {}
    for n, (j, m, r) in enumerate(order):
        bank, _, width = runs[j, m][r]
        mine = range(bank, bank + -(-width // 512))
        freed[j, m, r] = max([last_in.get(x, -1) for x in mine]) + 1
        last_in.update({x: n for x in mine})
    GROUPS = sum(banks_of(j) for j in range(STEPS))
    GROUP_AT = {(j, g): sum(banks_of(i) for i in range(j)) + g for j in range(STEPS) for g in range(banks_of(j))}
    assert GROUPS % 2 == 0

    def tiles_in(j, g):
        return min(GROUP, j + 1 - g * GROUP)

    with ExitStack() as ctx:
        a = Alloc(nc, ctx, "att")
        q_hl = [a.sb(f"q_hl{b}", [P, 2, SEQ], F32R) for b in range(2)]
        q_lh = [a.sb(f"q_lh{b}", [P, 2, SEQ], F32R) for b in range(2)]
        k_hl = [a.sb(f"k_hl{b}", [P, 2, SEQ], F32R) for b in range(2)]
        v_hi = [a.sb(f"v_hi{b}", [P, STEPS, P], F32R) for b in range(2)]
        v_lo = [a.sb(f"v_lo{b}", [P, STEPS, P], F32R) for b in range(2)]
        early = a.sb("early", [P, P], F32R)
        late = a.sb("late", [P, P], F32R)
        lams = a.sb("lams", [P, 4, DH])
        lam_dots = a.sb("lam_dots", [P, 2])
        lam_exps = a.sb("lam_exps", [P, 2])
        neg_lam = a.sb("neg_lam", [P, 1])
        g_col = a.sb("g_col", [P, 1])
        expo = [a.sb(f"expo{b}", [P, 2, SEQ]) for b in range(2)]
        neg_max = a.sb("neg_max", [P, 2, 2, 2])
        row_sum = a.sb("row_sum", [P, 2, 2, 2])
        total = a.sb("total", [P, 2, 2])
        inv = a.sb("inv", [P, 2, 2])
        ratio = a.sb("ratio", [P, 2])
        wt_hi = [a.sb(f"wt_hi{b}", [P, 512], F32R) for b in range(2)]
        wt_lo = [a.sb(f"wt_lo{b}", [P, 512], F32R) for b in range(2)]
        o_all = a.sb("o_all", [P, STEPS, P])
        o_sq = a.sb("o_sq", [P, P])
        o_sumsq = a.sb("o_sumsq", [P, STEPS])
        o_rms = a.sb("o_rms", [P, STEPS])
        o_rrms = a.sb("o_rrms", [P, STEPS])
        o_turned = a.sb("o_turned", [P, SEQ])
        ring = ctx.enter_context(nc.psum_tensor("att_ring", [P, RING * 512], F32))
        turned = [a.bank(f"turned{b}") for b in range(2)]
        out_bank = a.bank("out")

        waited = a.sem("waited")
        small_in = a.sem("small_in")
        chain = a.sem("chain")
        lam_exp_made = a.sem("lam_exp_made")
        head_in = [a.sem(f"head_in{b}") for b in range(2)]
        masks_made = a.sem("masks_made")
        scored = a.sem("scored")
        run_max = a.sem("run_max")
        max_made = a.sem("max_made")
        exp_made = a.sem("exp_made")
        total_made = a.sem("total_made")
        inv_made = a.sem("inv_made")
        ratio_made = a.sem("ratio_made")
        combined = a.sem("combined")
        group_turned = a.sem("group_turned")
        group_hi = a.sem("group_hi")
        group_lo = a.sem("group_lo")
        group_used = a.sem("group_used")
        o_read = a.sem("o_read")
        o_squared = a.sem("o_squared")
        o_rms_made = a.sem("o_rms_made")
        o_rrms_made = a.sem("o_rrms_made")
        o_normed = a.sem("o_normed")
        o_turn_done = a.sem("o_turn_done")
        o_staged = a.sem("o_staged")
        o_stored = Count(a.sem("o_stored"), 16)
        head_done = Count(a.sem("head_done"), 1)
        block = ctx.enter_context(nc.Block())
        HEAD_DMAS = 8

        @block.sync
        def _(sp):
            for n, vec in enumerate(lambdas):
                sp.dma_start(lams[:, n, :], vec.partition_broadcast(P)).then_inc(small_in, 16)
            sp.dma_start(g_col[:], subln_g.rearrange("(p o) -> p o", o=1)).then_inc(small_in, 16)

            def load_head(h, par):
                def rows(name, base):
                    return mid[name][bass.ds(h * P + base, P), :].rearrange("(m p) n -> p m n", p=DH)

                low, high = slice(0, DH), slice(DH, P)
                sp.dma_start(q_hl[par][low].bitcast(F32), rows("qk_hi", 0)).then_inc(head_in[par], 16)
                sp.dma_start(q_hl[par][high].bitcast(F32), rows("qk_lo", 0)).then_inc(head_in[par], 16)
                sp.dma_start(k_hl[par][low].bitcast(F32), rows("qk_hi", W)).then_inc(head_in[par], 16)
                sp.dma_start(k_hl[par][high].bitcast(F32), rows("qk_lo", W)).then_inc(head_in[par], 16)
                sp.dma_start(q_lh[par][low].bitcast(F32), rows("qk_lo", 0)).then_inc(head_in[par], 16)
                sp.dma_start(q_lh[par][high].bitcast(F32), rows("qk_hi", 0)).then_inc(head_in[par], 16)
                for name, tile in (("v_hi", v_hi), ("v_lo", v_lo)):
                    src = mid[name][:, bass.ds(h * P, P)].rearrange("(t p) n -> p t n", p=P)
                    sp.dma_start(tile[par][:].bitcast(F32), src).then_inc(head_in[par], 16)

            load_head(0, 0)
            with sp.Fori(0, HEADS // 2) as i:
                for p in range(2):
                    h = 2 * i + p
                    head_done.wait(sp, h)
                    sp.sem_inc(waited, 1)
                    load_head(2 * i + 1 if p == 0 else (1 - i) * 2, 1 - p)
                    for c in range(SEQ // 512):
                        sp.wait_ge(o_staged, h * (SEQ // 512) + c + 1)
                        sp.sem_inc(waited, 1)
                        sp.dma_start(mix[bass.ds(h * P, P), c * 512:(c + 1) * 512], o_turned[:, c * 512:(c + 1) * 512]).then_inc(o_stored.sem, 16)
            o_stored.wait(sp, 16 * HEADS * (SEQ // 512))
            for par in range(2):
                sp.wait_ge(head_in[par], 16 * HEAD_DMAS * (HEADS // 2 + (1 - par)))

        @block.scalar
        def _(act):
            def exponentiate(h, j, m):
                for r, (bank, key, width) in enumerate(runs[j, m]):
                    act.wait_ge(max_made, h * (2 * STEPS) + 2 * j + m + 1)
                    nc.scalar.activation(expo[j % 2][:, m, key:key + width], ring[:, bank * 512:bank * 512 + width], ACT.Exp,
                                         bias=neg_max[:, j % 2, m, 0:1],
                                         accum_out=row_sum[:, j % 2, r, m:m + 1]).then_inc(exp_made, 1)

            def group_high(h, i, j, g):
                k, n = GROUP_AT[j, g], tiles_in(j, g) * P
                act.wait_ge(group_turned, h * GROUPS + k + 1)
                if k >= 2:
                    act.wait_ge(group_used, h * GROUPS + k - 1)
                nc.scalar.activation(wt_hi[k % 2][:, 0:n], turned[k % 2][:, 0:n], ACT.Copy).then_inc(group_hi, 1)

            def read_output(h, j):
                act.wait_ge(group_used, h * GROUPS + GROUP_AT[j, banks_of(j) - 1] + 1)
                nc.scalar.activation(o_all[:, j, :], out_bank[:, 0:P], ACT.Copy, scale=inv[:, j % 2, 0:1]).then_inc(o_read, 1)
                act.wait_ge(o_read, h * STEPS + j + 1)
                if j:
                    act.wait_ge(o_squared, h * STEPS + j)
                nc.scalar.activation(o_sq[:], o_all[:, j, :], ACT.Square, accum_out=o_sumsq[:, j:j + 1]).then_inc(o_squared, 1)

            act.wait_ge(chain, 2)
            nc.scalar.activation(lam_exps[:], lam_dots[:], ACT.Exp).then_inc(lam_exp_made, 1)
            with act.Fori(0, HEADS // 2) as i:
                for p in range(2):
                    h = 2 * i + p
                    for j in range(STEPS + 1):
                        groups = range(banks_of(j - 1)) if j else ()
                        if j < STEPS:
                            exponentiate(h, j, 0)
                        if j >= 2:
                            read_output(h, j - 2)
                        for g in groups[:2]:
                            group_high(h, i, j - 1, g)
                        if j < STEPS:
                            exponentiate(h, j, 1)
                        for g in groups[2:]:
                            group_high(h, i, j - 1, g)
                    read_output(h, STEPS - 1)
                    act.wait_ge(o_squared, h * STEPS + STEPS)
                    nc.scalar.activation(o_rms[:], o_sumsq[:], ACT.Sqrt, bias=eps[:], scale=1.0 / P).then_inc(o_rms_made, 1)
                    o_stored.wait(act, h * (16 * SEQ // 512))
                    for c in range(SEQ // 512):
                        act.wait_ge(o_turn_done, h * (SEQ // 512) + c + 1)
                        nc.scalar.activation(o_turned[:, c * 512:(c + 1) * 512], turned[c % 2][:], ACT.Copy, scale=g_col[:]).then_inc(o_staged, 1)

        @block.vector
        def _(dve):
            def maximum(h, j, m):
                for r, (bank, key, width) in enumerate(runs[j, m]):
                    dve.wait_ge(scored, h * RUNS + RUN_AT[j, m, r] + 1)
                    last = nc.vector.tensor_reduce(neg_max[:, j % 2, m, r:r + 1], ring[:, bank * 512:bank * 512 + width], AX.X, ALU.max, negate=True)
                    if len(runs[j, m]) > 1:
                        last.then_inc(run_max, 1)
                if len(runs[j, m]) > 1:
                    dve.wait_ge(run_max, h * SPLIT_RUNS + split_runs(j, m))
                    last = nc.vector.tensor_tensor(neg_max[:, j % 2, m, 0:1], neg_max[:, j % 2, m, 0:1], neg_max[:, j % 2, m, 1:2], ALU.min)
                last.then_inc(max_made, 1)

            def split_runs(j, m):
                return sum(len(runs[key]) for key in runs if key <= (j, m) and len(runs[key]) > 1)

            SPLIT_RUNS = split_runs(STEPS, 0)

            def combine(h, j):
                b = j % 2
                dve.wait_ge(exp_made, h * RUNS + RUN_AT[j, 1, len(runs[j, 1]) - 1] + 1)
                n_runs = [len(runs[j, m]) for m in range(2)]
                for m in range(2):
                    if n_runs[m] == 2:
                        last = nc.vector.tensor_tensor(total[:, b, m:m + 1], row_sum[:, b, 0, m:m + 1], row_sum[:, b, 1, m:m + 1], ALU.add)
                    else:
                        last = nc.vector.tensor_copy(total[:, b, m:m + 1], row_sum[:, b, 0, m:m + 1])
                    last.then_inc(total_made, 1)
                dve.wait_ge(total_made, (h * STEPS + j + 1) * 2)
                nc.vector.reciprocal(inv[:, b, :], total[:, b, :]).then_inc(inv_made, 1)
                dve.wait_ge(inv_made, h * STEPS + j + 1)
                nc.vector.scalar_tensor_tensor(out=ratio[:, b:b + 1], in0=total[:, b, 0:1], scalar=neg_lam[:],
                                               in1=inv[:, b, 1:2], op0=ALU.mult, op1=ALU.mult).then_inc(ratio_made, 1)
                dve.wait_ge(ratio_made, h * STEPS + j + 1)
                n = (j + 1) * P
                nc.vector.scalar_tensor_tensor(out=expo[b][:, 0, 0:n], in0=expo[b][:, 1, 0:n], scalar=ratio[:, b:b + 1],
                                               in1=expo[b][:, 0, 0:n], op0=ALU.mult, op1=ALU.add).then_inc(combined, 1)

            def group_low(h, j, g):
                k, n = GROUP_AT[j, g], tiles_in(j, g) * P
                dve.wait_ge(group_hi, h * GROUPS + k + 1)
                nc.vector.tensor_tensor(wt_lo[k % 2][:, 0:n], turned[k % 2][:, 0:n], wt_hi[k % 2][:, 0:n].bitcast(F32), ALU.subtract).then_inc(group_lo, 1)

            for count in (o_stored, head_done):
                dve.sem_inc(count.sem, count.credit)
            nc.vector.memset(early[:].bitcast(F32), 0.0).then_inc(masks_made, 1)
            nc.vector.memset(late[:].bitcast(F32), 0.0).then_inc(masks_made, 1)
            dve.wait_ge(masks_made, 2)
            nc.vector.memset(early[0:1, 0:P // 2].bitcast(F32), 1.0).then_inc(masks_made, 1)
            nc.vector.memset(late[0:1, P // 2:P].bitcast(F32), MASKED).then_inc(masks_made, 1)
            dve.wait_ge(small_in, 16 * 5)
            for n in range(2):
                nc.vector.tensor_tensor_reduce(out=lams[:, 2 * n, :], in0=lams[:, 2 * n, :], in1=lams[:, 2 * n + 1, :], scale=1.0,
                                               scalar=0.0, op0=ALU.mult, op1=ALU.add, accum_out=lam_dots[:, n:n + 1]).then_inc(chain, 1)
            nc.vector.tensor_scalar(g_col[:], g_col[:], 1.0 - LAM_INIT, None, ALU.mult).then_inc(chain, 1)
            dve.wait_ge(lam_exp_made, 1)
            nc.vector.tensor_tensor(neg_lam[:], lam_exps[:, 1:2], lam_exps[:, 0:1], ALU.subtract).then_inc(chain, 1)
            dve.wait_ge(chain, 4)
            nc.vector.tensor_scalar(neg_lam[:], neg_lam[:], -LAM_INIT, None, ALU.add).then_inc(chain, 1)
            dve.wait_ge(chain, 5)
            with dve.Fori(0, HEADS // 2) as i:
                for p in range(2):
                    h = 2 * i + p
                    for j in range(STEPS + 1):
                        groups = range(banks_of(j - 1)) if j else ()
                        if j < STEPS:
                            maximum(h, j, 0)
                        if j:
                            combine(h, j - 1)
                        for g in groups[:2]:
                            group_low(h, j - 1, g)
                        if j < STEPS:
                            maximum(h, j, 1)
                        for g in groups[2:]:
                            group_low(h, j - 1, g)
                    dve.wait_ge(o_rms_made, h + 1)
                    nc.vector.reciprocal(o_rrms[:], o_rms[:]).then_inc(o_rrms_made, 1)
                    dve.wait_ge(o_rrms_made, h + 1)
                    for j in range(STEPS):
                        nc.vector.tensor_scalar(o_all[:, j, :], o_all[:, j, :], o_rrms[:, j:j + 1], None, ALU.mult).then_inc(o_normed, 1)

        @block.tensor
        def _(pe):
            def score(h, p, j, m):
                q = slice(j * P, (j + 1) * P)
                for r, (bank, key, width) in enumerate(runs[j, m]):
                    if freed[j, m, r]:
                        pe.wait_ge(exp_made, h * RUNS + freed[j, m, r])
                    for k in range(key, key + width, 512):
                        n = min(512, key + width - k)
                        at = bank * 512 + k - key
                        dst, keys = ring[:, at:at + n], k_hl[p][:, m, k:k + n]
                        diagonal = k + n == (j + 1) * P
                        pe.matmul(dst, q_hl[p][:, m, q], keys, start=True, stop=False)
                        if diagonal:
                            pe.matmul(ring[:, at + n - P:at + n], early[:], late[:], start=False, stop=False, skip_group_check=True)
                        last = pe.matmul(dst, q_lh[p][:, m, q], keys, start=False, stop=True)
                    last.then_inc(scored, 1)

            def turn(h, j, g):
                k = GROUP_AT[j, g]
                if g == 0:
                    pe.wait_ge(combined, h * STEPS + j + 1)
                if k >= 2:
                    pe.wait_ge(group_lo, h * GROUPS + k - 1)
                for t in range(tiles_in(j, g)):
                    key = (g * GROUP + t) * P
                    last = pe.transpose(turned[k % 2][:, t * P:(t + 1) * P], expo[j % 2][:, 0, key:key + P], ident[:])
                last.then_inc(group_turned, 1)

            def weigh(h, p, j, g):
                k = GROUP_AT[j, g]
                pe.wait_ge(group_lo, h * GROUPS + k + 1)
                if g == 0 and j:
                    pe.wait_ge(o_read, h * STEPS + j)
                for t in range(tiles_in(j, g)):
                    kt = g * GROUP + t
                    hi, lo = wt_hi[k % 2][:, t * P:(t + 1) * P], wt_lo[k % 2][:, t * P:(t + 1) * P]
                    pe.matmul(out_bank[:, 0:P], hi, v_hi[p][:, kt, :], start=kt == 0, stop=False)
                    pe.matmul(out_bank[:, 0:P], hi, v_lo[p][:, kt, :], start=False, stop=False)
                    last = pe.matmul(out_bank[:, 0:P], lo, v_hi[p][:, kt, :], start=False, stop=kt == j)
                last.then_inc(group_used, 1)

            pe.wait_ge(masks_made, 4)
            with pe.Fori(0, HEADS // 2) as i:
                for p in range(2):
                    h = 2 * i + p
                    pe.wait_ge(head_in[p], i * (16 * HEAD_DMAS) + 16 * HEAD_DMAS)
                    for j in range(STEPS + 1):
                        groups = banks_of(j - 1) if j else 0
                        if j < STEPS:
                            score(h, p, j, 0)
                        for g in range(min(2, groups)):
                            turn(h, j - 1, g)
                        if j < STEPS:
                            score(h, p, j, 1)
                        for g in range(groups):
                            weigh(h, p, j - 1, g)
                            if g + 2 < groups:
                                turn(h, j - 1, g + 2)
                    for c in range(SEQ // 512):
                        pe.wait_ge(o_normed, h * STEPS + (c + 1) * GROUP)
                        if c >= 2:
                            pe.wait_ge(o_staged, h * (SEQ // 512) + c - 1)
                        for t in range(GROUP):
                            last = pe.transpose(turned[c % 2][:, t * P:(t + 1) * P], o_all[:, c * GROUP + t, :], ident[:])
                        last.then_inc(o_turn_done, 1)
                    pe.wait_ge(o_turn_done, h * (SEQ // 512) + SEQ // 512)
                    pe.sem_inc(head_done.sem, 1)


def recur(nc, mid, norm_g, ident, eps, mix):
    C = P
    LEVELS = C.bit_length() - 1
    CH = TB // C
    HALF = HEADS // 2
    HC = HALF * CH
    RUN = C // 2

    with ExitStack() as ctx:
        a = Alloc(nc, ctx, "rec")
        q = [a.sb(f"q{b}", [P, HEADS, TB]) for b in range(2)]
        k = [a.sb(f"k{b}", [P, HEADS, TB]) for b in range(2)]
        f = [a.sb(f"f{b}", [P, HEADS, TB]) for b in range(2)]
        v = [a.sb(f"v{b}", [P, CH, W]) for b in range(2)]
        gate = [a.sb(f"gate{b}", [P, CH, W]) for b in range(2)]
        whole = [None] + [a.sb(f"whole{m}", [P, HEADS * TB >> m]) for m in range(1, LEVELS + 1)]
        mask = a.sb("mask", [P, LEVELS, HC, RUN])
        score = a.sb("score", [P, HEADS, CH, C])
        k_tok = a.sb("k_tok", [P, CH, HEADS, C])
        state = a.sb("state", [P, HEADS, C])
        o = a.sb("o", [P, CH, W])
        o_sq = a.sb("o_sq", [P, CH, W])
        o_sumsq = a.sb("o_sumsq", [P, CH, HEADS])
        o_rms = a.sb("o_rms", [P, CH * HEADS])
        o_rrms = a.sb("o_rrms", [P, CH * HEADS])
        g_col = a.sb("g_col", [P, 1])
        o_turned = a.sb("o_turned", [P, HEADS, TB])
        level_bank = [[a.bank(f"level{h}{n}") for n in range(2)] for h in range(2)]
        k_bank, o_bank, state_bank, turn_bank = (a.bank(f"{n}_bank") for n in ("k", "o", "state", "turn"))

        waited = a.sem("waited")
        gain_in = a.sem("gain_in")
        mask_made = a.sem("mask_made")
        block_in = [a.sem(f"block_in{b}") for b in range(2)]
        whole_made = a.sem("whole_made")
        raw_scored = a.sem("raw_scored")
        q_ready = [a.sem(f"q_ready{h}") for h in range(2)]
        k_ready = [a.sem(f"k_ready{h}") for h in range(2)]
        level_scored = [a.sem(f"level_scored{h}") for h in range(2)]
        level_read = [a.sem(f"level_read{h}") for h in range(2)]
        k_turned = a.sem("k_turned")
        k_tok_made = a.sem("k_tok_made")
        o_done = a.sem("o_done")
        added = a.sem("added")
        state_made = Count(a.sem("state_made"), 1)
        o_copied = Count(a.sem("o_copied"), 1)
        o_squared = a.sem("o_squared")
        o_summed = a.sem("o_summed")
        o_rms_made = a.sem("o_rms_made")
        o_rrms_made = a.sem("o_rrms_made")
        o_scaled = a.sem("o_scaled")
        o_gated = a.sem("o_gated")
        o_turn_done = a.sem("o_turn_done")
        o_staged = a.sem("o_staged")
        o_stored = Count(a.sem("o_stored"), 16)
        block_done = Count(a.sem("block_done"), 1)
        block = ctx.enter_context(nc.Block())
        BLOCK_DMAS = 5
        UPDATES = LEVELS + 1

        def half(t, h):
            return t[:, h * HALF:(h + 1) * HALF, :].rearrange("p h n -> p (h n)")

        def runs(t, h, m, side):
            return half(t, h).rearrange("p (n s j) -> p n s j", s=2, j=1 << m)[:, :, side, :]

        def factor(B, p, h, m, side):
            pairs = HC * (C >> m + 1)
            src = half(f[p], h) if m == 0 else whole[m][:, h * 2 * pairs:(h + 1) * 2 * pairs]
            return src.rearrange("p (n s) -> p n s", s=2)[:, :, 1 - side].unsqueeze(2).to_broadcast([P, pairs, 1 << m])

        @block.sync
        def _(sp):
            sp.dma_start(g_col[:], norm_g.rearrange("(p o) -> p o", o=1)).then_inc(gain_in, 16)

            def load_block(tok, par):
                for t, name in ((q, "hq"), (k, "hk"), (f, "hf")):
                    sp.dma_start(t[par][:], mid[name][:, bass.ds(tok, TB)].rearrange("(h p) n -> p h n", p=P)).then_inc(block_in[par], 16)
                for t, name in ((v, "hv"), (gate, "hgate")):
                    sp.dma_start(t[par][:], mid[name][bass.ds(tok, TB), :].rearrange("(c p) n -> p c n", p=P)).then_inc(block_in[par], 16)

            load_block(0, 0)
            with sp.Fori(0, BLOCKS // 2) as i:
                for p in range(2):
                    B = 2 * i + p
                    block_done.wait(sp, B)
                    sp.sem_inc(waited, 1)
                    load_block((2 * i + 1) * TB if p == 0 else (1 - i) * 2 * TB, 1 - p)
                    sp.wait_ge(o_staged, (B + 1) * HEADS)
                    sp.sem_inc(waited, 1)
                    sp.dma_start(mix[W:2 * W, bass.ds(B * TB, TB)].rearrange("(h p) n -> p h n", p=P), o_turned[:]).then_inc(o_stored.sem, 16)
            o_stored.wait(sp, 16 * BLOCKS)
            for par in range(2):
                sp.wait_ge(block_in[par], 16 * BLOCK_DMAS * (BLOCKS // 2 + (1 - par)))

        @block.gpsimd
        def _(pool):
            nc.gpsimd.memset(mask[:], 1.0).then_inc(mask_made, 1)
            for m in range(LEVELS):
                j = 1 << m
                view = mask[:, m].rearrange("p a (n j) -> p a n j", j=j)
                for base, sign, end in ((0, 1, 0), (j - 1, -1, 1)):
                    pool.wait_ge(mask_made, 2 * m + end + 1)
                    nc.gpsimd.affine_select(out=view, in_=view, compare_op=ALU.is_ge, fill=0.0, base=base,
                                            pattern=[[0, HC], [-sign * 2 * j, C // (2 * j)], [0, j]],
                                            channel_multiplier=sign).then_inc(mask_made, 1)
            with pool.Fori(0, BLOCKS // 2) as i:
                for p in range(2):
                    B = 2 * i + p
                    for m in range(LEVELS):
                        pool.wait_ge(whole_made, B * LEVELS + m + 1)
                        for h in range(2):
                            pool.wait_ge(level_scored[h], B * LEVELS + m + 1)
                            pool.sem_inc(waited, 1)
                            nc.gpsimd.tensor_tensor(runs(k[p], h, m, 0), runs(k[p], h, m, 0), factor(B, p, h, m, 0), ALU.mult).then_inc(k_ready[h], 1)

        @block.scalar
        def _(act):
            act.wait_ge(gain_in, 16)
            with act.Fori(0, BLOCKS // 2) as i:
                for p in range(2):
                    B = 2 * i + p
                    for c in range(CH):
                        act.wait_ge(k_turned, B * CH + c + 1)
                        nc.scalar.activation(k_tok[:, c].rearrange("p h n -> p (h n)"), k_bank[:], ACT.Copy).then_inc(k_tok_made, 1)
                    for c in range(CH):
                        act.wait_ge(o_done, B * CH + c + 1)
                        nc.scalar.activation(o_sq[:, c], o_bank[:], ACT.Square).then_inc(o_squared, 1)
                        nc.scalar.activation(o[:, c], o_bank[:], ACT.Copy).then_inc(o_copied.sem, 1)
                    act.wait_ge(o_summed, B + 1)
                    nc.scalar.activation(o_rms[:], o_sumsq[:].rearrange("p c h -> p (c h)"), ACT.Sqrt, bias=eps[:], scale=1.0 / C).then_inc(o_rms_made, 1)
                    o_stored.wait(act, B * 16)
                    for h in range(HEADS):
                        act.wait_ge(o_turn_done, B * HEADS + h + 1)
                        nc.scalar.activation(o_turned[:, h, :], turn_bank[:], ACT.Copy, scale=g_col[:]).then_inc(o_staged, 1)

        @block.vector
        def _(dve):
            for count in (state_made, o_copied, o_stored, block_done):
                dve.sem_inc(count.sem, count.credit)
            nc.vector.memset(state[:], 0.0).then_inc(added, 1)
            dve.wait_ge(added, 1)
            dve.wait_ge(mask_made, 2 * LEVELS + 1)
            with dve.Fori(0, BLOCKS // 2) as i:
                for p in range(2):
                    B = 2 * i + p
                    dve.wait_ge(block_in[p], i * (16 * BLOCK_DMAS) + 16 * BLOCK_DMAS)
                    for h in range(2):
                        dve.wait_ge(raw_scored, B * 2 + h + 1)
                        nc.vector.tensor_tensor(half(q[p], h), half(q[p], h), half(f[p], h), ALU.mult).then_inc(q_ready[h], 1)
                        for n in range(2):
                            last = nc.vector.tensor_tensor(score[:, h * HALF + n], level_bank[h][n][:].rearrange("p (c t) -> p c t", t=C),
                                                           ident[:].unsqueeze(1).to_broadcast([P, CH, C]), ALU.mult)
                            last.then_inc(level_read[h], 1)
                    for m in range(LEVELS):
                        src = f[p][:].rearrange("p h n -> p (h n)") if m == 0 else whole[m][:]
                        src = src.rearrange("p (n s) -> p n s", s=2)
                        if m:
                            dve.wait_ge(whole_made, B * LEVELS + m)
                        nc.vector.tensor_tensor(whole[m + 1][:], src[:, :, 0], src[:, :, 1], ALU.mult).then_inc(whole_made, 1)
                    dve.wait_ge(whole_made, B * LEVELS + LEVELS)
                    for m in range(LEVELS):
                        for h in range(2):
                            dve.wait_ge(level_scored[h], B * LEVELS + m + 1)
                            dve.wait_ge(q_ready[h], B * UPDATES + m + 1)
                            nc.vector.tensor_tensor(runs(q[p], h, m, 1), runs(q[p], h, m, 1), factor(B, p, h, m, 1), ALU.mult).then_inc(q_ready[h], 1)
                            dst = score[:, h * HALF:(h + 1) * HALF].rearrange("p h c (n s j) -> p (h c n) s j", s=2, j=1 << m)[:, :, 1, :]
                            dve.wait_ge(level_read[h], B * (2 + LEVELS) + m + 2)
                            dve.sem_inc(waited, 1)
                            nc.vector.copy_predicated(dst, mask[:, m].rearrange("p a (n j) -> p (a n) j", j=1 << m).bitcast(mybir.dt.uint32),
                                                      level_bank[h][m % 2][:].rearrange("p (n j) -> p n j", j=1 << m)).then_inc(level_read[h], 1)
                    for c in range(CH):
                        dve.wait_ge(added, B * CH + c + 2)
                        dve.wait_ge(o_done, B * CH + c + 1)
                        state_made.wait(dve, B * (CH * HEADS) + c * HEADS)
                        for h in range(HEADS):
                            nc.vector.scalar_tensor_tensor(out=state[:, h, :], in0=state[:, h, :], scalar=whole[LEVELS][:, h * CH + c:h * CH + c + 1],
                                                           in1=state_bank[:, h * C:(h + 1) * C], op0=ALU.mult, op1=ALU.add).then_inc(state_made.sem, 1)
                    dve.wait_ge(o_squared, B * CH + CH)
                    nc.vector.tensor_reduce(o_sumsq[:].rearrange("p c h -> p (c h)"), o_sq[:].rearrange("p c (h n) -> p (c h) n", n=C), AX.X, ALU.add).then_inc(o_summed, 1)
                    dve.wait_ge(o_rms_made, B + 1)
                    nc.vector.reciprocal(o_rrms[:], o_rms[:]).then_inc(o_rrms_made, 1)
                    dve.wait_ge(o_rrms_made, B + 1)
                    o_copied.wait(dve, B * CH + CH)
                    nc.vector.tensor_tensor(o[:].rearrange("p c (h n) -> p (c h) n", n=C), o[:].rearrange("p c (h n) -> p (c h) n", n=C),
                                            o_rrms[:].unsqueeze(2).to_broadcast([P, CH * HEADS, C]), ALU.mult).then_inc(o_scaled, 1)
                    dve.wait_ge(o_scaled, B + 1)
                    nc.vector.tensor_tensor(o[:], o[:], gate[p][:], ALU.mult).then_inc(o_gated, 1)

        @block.tensor
        def _(pe):
            with pe.Fori(0, BLOCKS // 2) as i:
                for p in range(2):
                    B = 2 * i + p
                    pe.wait_ge(block_in[p], i * (16 * BLOCK_DMAS) + 16 * BLOCK_DMAS)
                    for h in range(2):
                        for n in range(HALF):
                            for c in range(CH):
                                tok = slice(c * C, (c + 1) * C)
                                last = pe.matmul(level_bank[h][n][:, tok], k[p][:, h * HALF + n, tok], q[p][:, h * HALF + n, tok], start=True, stop=True)
                        last.then_inc(raw_scored, 1)
                    for m in range(LEVELS):
                        for h in range(2):
                            pe.wait_ge(q_ready[h], B * UPDATES + m + 1)
                            if m:
                                pe.wait_ge(k_ready[h], B * LEVELS + m)
                            pe.wait_ge(level_read[h], B * (2 + LEVELS) + (m + 1 if m else 1))
                            for n in range(HALF):
                                for c in range(CH):
                                    at = (n * CH + c) * RUN
                                    tok = slice(c * C, (c + 1) * C)
                                    queries = q[p][:, h * HALF + n, tok].rearrange("p (n s j) -> p n s j", s=2, j=1 << m)[:, :, 1, :]
                                    last = pe.matmul(level_bank[h][m % 2][:, at:at + RUN].rearrange("p (n j) -> p n j", j=1 << m),
                                                     k[p][:, h * HALF + n, tok], queries, start=True, stop=True)
                            last.then_inc(level_scored[h], 1)
                    for h in range(2):
                        pe.wait_ge(q_ready[h], B * UPDATES + UPDATES)
                        pe.wait_ge(k_ready[h], B * LEVELS + LEVELS)
                        pe.wait_ge(level_read[h], (B + 1) * (2 + LEVELS))
                    for c in range(CH):
                        tok = slice(c * C, (c + 1) * C)
                        if c:
                            pe.wait_ge(k_tok_made, B * CH + c)
                        for h in range(HEADS):
                            last = pe.transpose(k_bank[:, h * C:(h + 1) * C], k[p][:, h, tok], ident[:])
                        last.then_inc(k_turned, 1)
                    for c in range(CH):
                        tok = slice(c * C, (c + 1) * C)
                        o_copied.wait(pe, B * CH + c)
                        state_made.wait(pe, B * (CH * HEADS) + c * HEADS)
                        for h in range(HEADS):
                            mine = slice(h * C, (h + 1) * C)
                            pe.matmul(o_bank[:, mine], score[:, h, c], v[p][:, c, mine], start=True, stop=False)
                            last = pe.matmul(o_bank[:, mine], q[p][:, h, tok], state[:, h, :], start=False, stop=True)
                        last.then_inc(o_done, 1)
                        pe.wait_ge(k_tok_made, B * CH + c + 1)
                        for h in range(HEADS):
                            mine = slice(h * C, (h + 1) * C)
                            last = pe.matmul(state_bank[:, mine], k_tok[:, c, h, :], v[p][:, c, mine], start=True, stop=True)
                        last.then_inc(added, 1)
                    pe.wait_ge(o_gated, B + 1)
                    for h in range(HEADS):
                        if h:
                            pe.wait_ge(o_staged, B * HEADS + h)
                        for c in range(CH):
                            last = pe.transpose(turn_bank[:, c * C:(c + 1) * C], o[:, c, h * C:(h + 1) * C], ident[:])
                        last.then_inc(o_turn_done, 1)
                    pe.wait_ge(o_turn_done, (B + 1) * HEADS)
                    pe.sem_inc(block_done.sem, 1)


def feed(nc, x, mix, w_out, ffn_g, w_gate, w_up, w_down, ident, ones, eps, y):
    FS = D_FF // P
    OUTS = D // UC
    PAIRS = D_FF // UC
    CHUNKS = [range(s, min(s + KS, FS)) for s in range(0, FS, KS)]
    GATED = OUTS + 2 * PAIRS
    UNITS = GATED + OUTS * len(CHUNKS)
    assert UNITS % 2 == 0 and OUTS % 2 == 0

    with ExitStack() as ctx:
        a = Alloc(nc, ctx, "feed")
        g_col = a.sb("g_col", [P, KS])
        mix_raw = a.sb("mix_raw", [P, 2, TB])
        x_piece = a.sb("x_piece", [P, SUB, UC])
        x_mid = a.sb("x_mid", [P, KS, TB])
        h_hi = a.sb("h_hi", [P, KS, TB], F32R)
        h_lo = a.sb("h_lo", [P, KS, TB], F32R)
        w_raw = [a.sb(f"w_raw{b}", [P, KS, UC]) for b in range(2)]
        w_hi = [a.sb(f"w_hi{b}", [P, KS, UC], F32R) for b in range(2)]
        w_lo = [a.sb(f"w_lo{b}", [P, KS, UC], F32R) for b in range(2)]
        ff_hi = a.sb("ff_hi", [P, FS, TB], F32R)
        ff_lo = a.sb("ff_lo", [P, FS, TB], F32R)
        gate_work = a.sb("gate_work", [P, UT, TB])
        ff_work = a.sb("ff_work", [P, UT, TB])
        rms = a.sb("rms", [P, SUB])
        rrms = a.sb("rrms", [P, SUB])
        wide = a.sb("wide", [P, SUB, P])
        prod = [[a.bank(f"prod{b}{t}") for t in range(UT)] for b in range(2)]
        turned = [a.bank(f"turned{t}") for t in range(UT)]
        sums = a.bank("sums")
        scales = a.bank("scales")

        waited = a.sem("waited")
        pe_waited = a.sem("pe_waited")
        gains_in = a.sem("gains_in")
        mix_in = a.sem("mix_in")
        x_in = a.sem("x_in")
        w_in_sem = [a.sem(f"w_in{b}") for b in range(2)]
        w_hi_made = a.sem("w_hi_made")
        w_lo_made = a.sem("w_lo_made")
        unit_done = Count(a.sem("unit_done"), 1)
        mix_hi_made = a.sem("mix_hi_made")
        mix_lo_made = a.sem("mix_lo_made")
        x_mid_made = a.sem("x_mid_made")
        sq_made = a.sem("sq_made")
        sums_made = Count(a.sem("sums_made"), 1)
        rms_made = a.sem("rms_made")
        rrms_made = a.sem("rrms_made")
        widened = a.sem("widened")
        spread = a.sem("spread")
        h_made = a.sem("h_made")
        h_hi_made = a.sem("h_hi_made")
        h_lo_made = a.sem("h_lo_made")
        sigmoid_made = a.sem("sigmoid_made")
        gate_made = Count(a.sem("gate_made"), 1)
        ff_made = Count(a.sem("ff_made"), 1)
        ff_hi_made = a.sem("ff_hi_made")
        ff_lo_made = a.sem("ff_lo_made")
        y_made = a.sem("y_made")
        y_turned = a.sem("y_turned")
        y_staged = a.sem("y_staged")
        y_stored = Count(a.sem("y_stored"), 16)
        block = ctx.enter_context(nc.Block())

        mix_view = mix.rearrange("(s p) n -> p s n", p=P)
        views = {"out": w_out.rearrange("(s p) n -> p s n", p=P), "gate": w_gate.rearrange("(s p) n -> p s n", p=P),
                 "up": w_up.rearrange("(s p) n -> p s n", p=P), "down": w_down.rearrange("(s p) n -> p s n", p=P)}

        def after(b):
            return ((b + 1) % BLOCKS) * TB

        def store_y(sp, b, c):
            sp.wait_ge(y_staged, b * (OUTS * UT) + (c + 1) * UT)
            sp.sem_inc(waited, 1)
            for t in range(UT):
                dst = y[bass.ds(b * TB, TB), c * UC + t * P:c * UC + (t + 1) * P].rearrange("(s p) n -> p s n", p=P)
                sp.dma_start(dst, ff_work[:, t, :].rearrange("p (s n) -> p s n", s=SUB)).then_inc(y_stored.sem, 16)

        def slabs_of(n):
            n = n % UNITS
            return KS if n < GATED else len(CHUNKS[(n - GATED) % len(CHUNKS)])

        def stage_y(act, b, c):
            y_stored.wait(act, b * (16 * UT * OUTS) + 16 * UT * c)
            for t in range(UT):
                act.wait_ge(y_turned, b * KS + c * UT + t + 1)
                nc.scalar.activation(ff_work[:, t, :], turned[t][:], ACT.Copy).then_inc(y_staged, 1)

        def x_mid_normed(s):
            return ff_work[:, s % UT, :]

        def h_low(dve, b, s):
            dve.wait_ge(h_hi_made, b * KS + s + 1)
            nc.vector.tensor_tensor(h_lo[:, s, :], x_mid_normed(s), h_hi[:, s, :].bitcast(F32), ALU.subtract).then_inc(h_lo_made, 1)

        @block.sync
        def _(sp):
            def load_w(n, kind, column, slabs=range(KS)):
                slot = n % 2
                sp.dma_start(w_raw[slot][:, 0:len(slabs), :],
                             views[kind][:, slabs[0]:slabs[-1] + 1, bass.ds(column, UC)]).then_inc(w_in_sem[slot], 16)

            def load_down(d):
                c, j = divmod(d, len(CHUNKS))
                load_w(d, "down", c * UC, CHUNKS[j])

            def split_done(b, n):
                sp.wait_ge(w_lo_made, b * UNITS + n + 1)

            def load_mix(tok, c):
                sp.dma_start(mix_raw[:], mix_view[:, 2 * c:2 * c + 2, bass.ds(tok, TB)]).then_inc(mix_in, 16)

            def load_x(tok, u):
                sp.dma_start(x_piece[:], x[bass.ds(tok, TB), u * UC:(u + 1) * UC].rearrange("(t p) n -> p t n", p=P)).then_inc(x_in, 16)

            sp.dma_start(g_col[:], ffn_g.rearrange("(s p) -> p s", p=P), allow_slow_non_contiguous=True).then_inc(gains_in, 16)
            load_mix(0, 0)
            load_w(0, "out", 0)
            load_w(1, "out", UC)
            load_x(0, 0)
            for c in range(1, OUTS):
                sp.wait_ge(mix_lo_made, c)
                load_mix(0, c)
            with sp.Fori(0, BLOCKS) as b:
                for u in range(OUTS):
                    split_done(b, u)
                    if u + 2 < OUTS:
                        load_w(u, "out", (u + 2) * UC)
                    else:
                        load_w(u, ("gate", "up")[u + 2 - OUTS], 0)
                    if u + 1 < OUTS:
                        unit_done.wait(sp, b * UNITS + u + 1)
                        sp.sem_inc(waited, 1)
                        load_x(b * TB, u + 1)
                with sp.Fori(0, PAIRS - 1) as f:
                    for k, kind in enumerate(("gate", "up")):
                        sp.wait_ge(w_lo_made, b * UNITS + f * 2 + (OUTS + k + 1))
                        sp.sem_inc(waited, 1)
                        load_w(k, kind, f * UC + UC)
                for d in range(2):
                    split_done(b, GATED - 2 + d)
                    load_down(d)
                for d in range(OUTS * len(CHUNKS)):
                    c, j = divmod(d, len(CHUNKS))
                    split_done(b, GATED + d)
                    if d + 2 < OUTS * len(CHUNKS):
                        load_down(d + 2)
                    else:
                        load_w(d, "out", (d + 2 - OUTS * len(CHUNKS)) * UC)
                    if j == 0:
                        sp.wait_ge(mix_lo_made, b * OUTS + OUTS + c)
                        sp.sem_inc(waited, 1)
                        load_mix(after(b), c)
                        if c == 0:
                            load_x(after(b), 0)
                        else:
                            store_y(sp, b, c - 1)
                store_y(sp, b, OUTS - 1)
            y_stored.wait(sp, 16 * UT * OUTS * BLOCKS)
            sp.wait_ge(x_in, 16 * (OUTS * BLOCKS + 1))
            sp.wait_ge(mix_in, 16 * OUTS * (BLOCKS + 1))
            for slot in range(2):
                sp.wait_ge(w_in_sem[slot], 16 * (UNITS // 2 * BLOCKS + 1))

        @block.scalar
        def _(act):
            def split_w(count, in_count, slot, slabs=KS):
                act.wait_ge(w_in_sem[slot], in_count)
                unit_done.wait(act, count - 1)
                nc.scalar.activation(w_hi[slot][:, 0:slabs, :], w_raw[slot][:, 0:slabs, :], ACT.Copy).then_inc(w_hi_made, 1)

            def split_unit(b, n):
                split_w(b * UNITS + n, b * (UNITS // 2 * 16) + 16 * (n // 2 + 1), n % 2, slabs_of(n))

            def split_mix(count, c):
                act.wait_ge(mix_in, count * 16 + 16)
                nc.scalar.activation(h_hi[:, 2 * c:2 * c + 2, :], mix_raw[:], ACT.Copy).then_inc(mix_hi_made, 1)

            act.wait_ge(gains_in, 16)
            for c in range(OUTS):
                split_mix(c, c)
            act.wait_ge(w_in_sem[0], 16)
            nc.scalar.activation(w_hi[0][:], w_raw[0][:], ACT.Copy).then_inc(w_hi_made, 1)
            with act.Fori(0, BLOCKS) as b:
                for u in range(OUTS):
                    split_unit(b, u + 1)
                    unit_done.wait(act, b * UNITS + u + 1)
                    for t in range(UT):
                        nc.scalar.activation(x_mid[:, u * UT + t, :], prod[u % 2][t][:], ACT.Copy).then_inc(x_mid_made, 1)
                    sums_made.wait(act, b * OUTS + u)
                    for t in range(UT):
                        act.wait_ge(x_mid_made, b * KS + u * UT + t + 1)
                        nc.scalar.activation(gate_work[:, t, :], x_mid[:, u * UT + t, :], ACT.Square).then_inc(sq_made, 1)
                sums_made.wait(act, b * OUTS + OUTS)
                nc.scalar.activation(rms[:], sums[:, 0:SUB], ACT.Sqrt, bias=eps[:], scale=1.0 / D).then_inc(rms_made, 1)
                for s in range(KS):
                    act.wait_ge(h_made, b * KS + s + 1)
                    nc.scalar.activation(h_hi[:, s, :], x_mid_normed(s), ACT.Copy).then_inc(h_hi_made, 1)
                with act.Fori(0, PAIRS) as f:
                    split_w(b * UNITS + f * 2 + (OUTS + 1), b * (UNITS // 2 * 16) + f * 16 + (OUTS // 2 + 1) * 16, 1)
                    unit_done.wait(act, b * UNITS + f * 2 + (OUTS + 1))
                    for t in range(UT):
                        nc.scalar.activation(gate_work[:, t, :], prod[0][t][:], ACT.Sigmoid).then_inc(sigmoid_made, 1)
                    split_w(b * UNITS + f * 2 + (OUTS + 2), b * (UNITS // 2 * 16) + f * 16 + (OUTS // 2 + 2) * 16, 0)
                    for t in range(UT):
                        ff_made.wait(act, b * FS + f * UT + (t + 1))
                        nc.scalar.activation(ff_hi[:, bass.ds(f * UT + t, 1), :].rearrange("p o n -> p (o n)"),
                                             ff_work[:, t, :], ACT.Copy).then_inc(ff_hi_made, 1)
                for d in range(OUTS * len(CHUNKS)):
                    c, j = divmod(d, len(CHUNKS))
                    split_unit(b, GATED + d + 1)
                    if j == 0:
                        split_mix(b * OUTS + OUTS + c, c)
                    if c and j == 1 or d == OUTS * len(CHUNKS) - 1:
                        stage_y(act, b, c - 1 if j == 1 else c)

        @block.vector
        def _(dve):
            def split_w(count, slot, slabs=KS):
                dve.wait_ge(w_hi_made, count + 1)
                nc.vector.tensor_tensor(w_lo[slot][:, 0:slabs, :], w_raw[slot][:, 0:slabs, :],
                                        w_hi[slot][:, 0:slabs, :].bitcast(F32), ALU.subtract).then_inc(w_lo_made, 1)

            def split_mix(count, c):
                dve.wait_ge(mix_hi_made, count + 1)
                nc.vector.tensor_tensor(h_lo[:, 2 * c:2 * c + 2, :], mix_raw[:], h_hi[:, 2 * c:2 * c + 2, :].bitcast(F32),
                                        ALU.subtract).then_inc(mix_lo_made, 1)

            for count in (unit_done, gate_made, ff_made, sums_made, y_stored):
                dve.sem_inc(count.sem, count.credit)
            dve.wait_ge(gains_in, 16)
            for c in range(OUTS):
                split_mix(c, c)
            dve.wait_ge(w_hi_made, 1)
            nc.vector.tensor_tensor(w_lo[0][:], w_raw[0][:], w_hi[0][:].bitcast(F32), ALU.subtract).then_inc(w_lo_made, 1)
            with dve.Fori(0, BLOCKS) as b:
                for u in range(OUTS):
                    split_w(b * UNITS + u + 1, (u + 1) % 2)
                dve.wait_ge(rms_made, b + 1)
                nc.vector.reciprocal(rrms[:], rms[:]).then_inc(rrms_made, 1)
                dve.wait_ge(rrms_made, b + 1)
                nc.vector.tensor_copy(wide[:], rrms[:].unsqueeze(2).to_broadcast([P, SUB, P])).then_inc(widened, 1)
                dve.wait_ge(spread, b + 1)
                y_stored.wait(dve, b * (16 * UT * OUTS))
                for s in range(KS):
                    if s >= UT:
                        dve.wait_ge(h_lo_made, b * KS + s - UT + 1)
                    nc.vector.scalar_tensor_tensor(out=x_mid_normed(s), in0=x_mid[:, s, :], scalar=g_col[:, s:s + 1],
                                                   in1=scales[:], op0=ALU.mult, op1=ALU.mult).then_inc(h_made, 1)
                    if s:
                        h_low(dve, b, s - 1)
                h_low(dve, b, KS - 1)
                with dve.Fori(0, PAIRS) as f:
                    split_w(b * UNITS + f * 2 + (OUTS + 1), 1)
                    for t in range(UT):
                        dve.wait_ge(sigmoid_made, b * FS + f * UT + (t + 1))
                        nc.vector.tensor_tensor(gate_work[:, t, :], prod[0][t][:], gate_work[:, t, :], ALU.mult).then_inc(gate_made.sem, 1)
                    split_w(b * UNITS + f * 2 + (OUTS + 2), 0)
                    unit_done.wait(dve, b * UNITS + f * 2 + (OUTS + 2))
                    for t in range(UT):
                        gate_made.wait(dve, b * FS + f * UT + (t + 1))
                        nc.vector.tensor_tensor(ff_work[:, t, :], prod[1][t][:], gate_work[:, t, :], ALU.mult).then_inc(ff_made.sem, 1)
                    for t in range(UT):
                        slab = bass.ds(f * UT + t, 1)
                        dve.wait_ge(ff_hi_made, b * FS + f * UT + (t + 1))
                        nc.vector.tensor_tensor(ff_lo[:, slab, :].rearrange("p o n -> p (o n)"), ff_work[:, t, :],
                                                ff_hi[:, slab, :].rearrange("p o n -> p (o n)").bitcast(F32),
                                                ALU.subtract).then_inc(ff_lo_made, 1)
                for d in range(OUTS * len(CHUNKS)):
                    c, j = divmod(d, len(CHUNKS))
                    split_w(b * UNITS + GATED + d + 1, (d + 1) % 2, slabs_of(GATED + d + 1))
                    if j == 0:
                        split_mix(b * OUTS + OUTS + c, c)
                    if j == len(CHUNKS) - 1:
                        unit_done.wait(dve, b * UNITS + GATED + d + 1)
                        for t in range(UT):
                            s = c * UT + t
                            nc.vector.tensor_tensor(x_mid[:, s, :], prod[c % 2][t][:], x_mid[:, s, :], ALU.add).then_inc(y_made, 1)

        @block.tensor
        def _(pe):
            def product(dst, slot, col, slabs, hi, lo, first, stop):
                for k, s in enumerate(slabs):
                    pe.matmul(dst, w_hi[slot][:, k, col], hi[:, s, :], start=first and k == 0, stop=False)
                    pe.matmul(dst, w_hi[slot][:, k, col], lo[:, s, :], start=False, stop=False)
                    last = pe.matmul(dst, w_lo[slot][:, k, col], hi[:, s, :], start=False,
                                     stop=stop and k == len(slabs) - 1)
                return last

            def sum_squares(b, u):
                for t in range(UT):
                    pe.wait_ge(sq_made, b * KS + u * UT + t + 1)
                    for r in range(SUB):
                        last = pe.matmul(sums[:, r:r + 1], gate_work[:, t, r * P:(r + 1) * P], ones[:, 0:1],
                                         start=u == 0 and t == 0 and r == 0, stop=u == OUTS - 1 and t == UT - 1,
                                         skip_group_check=True)
                last.then_inc(sums_made.sem, 1)

            def turn_y(b, c):
                for t in range(UT):
                    s = c * UT + t
                    pe.wait_ge(y_made, b * KS + s + 1)
                    if c:
                        pe.wait_ge(y_staged, b * KS + s - UT + 1)
                    for r in range(SUB):
                        last = pe.transpose(turned[t][:, r * P:(r + 1) * P], x_mid[:, s, r * P:(r + 1) * P], ident[:])
                    last.then_inc(y_turned, 1)

            with pe.Fori(0, BLOCKS) as b:
                pe.wait_ge(mix_lo_made, b * OUTS + OUTS)
                for u in range(OUTS):
                    pe.wait_ge(w_lo_made, b * UNITS + u + 1)
                    if u >= 2:
                        pe.wait_ge(x_mid_made, b * KS + (u - 1) * UT)
                    for t in range(UT):
                        col = slice(t * P, (t + 1) * P)
                        product(prod[u % 2][t][:], u % 2, col, range(KS), h_hi, h_lo, True, False)
                        if t == 0:
                            pe.wait_ge(x_in, b * (16 * OUTS) + 16 * (u + 1))
                            if u:
                                sum_squares(b, u - 1)
                        for r in range(SUB):
                            last = pe.matmul(prod[u % 2][t][:, r * P:(r + 1) * P], x_piece[:, r, col], ident[:],
                                             start=False, stop=r == SUB - 1)
                    last.then_inc(unit_done.sem, 1)
                sum_squares(b, OUTS - 1)
                pe.wait_ge(widened, b + 1)
                for r in range(SUB):
                    last = pe.matmul(scales[:, r * P:(r + 1) * P], wide[:, r, :], ident[:], start=True, stop=True)
                last.then_inc(spread, 1)
                pe.wait_ge(h_lo_made, b * KS + KS)
                pe.sem_inc(pe_waited, 1)
                with pe.Fori(0, PAIRS) as f:
                    for k in range(2):
                        pe.wait_ge(w_lo_made, b * UNITS + f * 2 + (OUTS + k + 1))
                        (gate_made, ff_made)[k].wait(pe, b * FS + f * UT)
                        for t in range(UT):
                            last = product(prod[k][t][:], k, slice(t * P, (t + 1) * P), range(KS), h_hi, h_lo, True, True)
                        last.then_inc(unit_done.sem, 1)
                for d in range(OUTS * len(CHUNKS)):
                    c, j = divmod(d, len(CHUNKS))
                    n, slabs = GATED + d, CHUNKS[j]
                    pe.wait_ge(w_lo_made, b * UNITS + n + 1)
                    if d == 0:
                        gate_made.wait(pe, b * FS + FS)
                    if c == 0:
                        pe.wait_ge(ff_lo_made, b * FS + slabs[-1] + 1)
                    for t in range(UT):
                        last = product(prod[c % 2][t][:], n % 2, slice(t * P, (t + 1) * P), slabs, ff_hi, ff_lo,
                                       j == 0, j == len(CHUNKS) - 1)
                        if c and j == 0 and t == 0:
                            turn_y(b, c - 1)
                    last.then_inc(unit_done.sem, 1)
                turn_y(b, OUTS - 1)


def hybrid_trunk_kernel(nc, x, attn_norm_g, w_in, q_norm_g, k_norm_g, lambda_q1, lambda_k1, lambda_q2, lambda_k2,
                        subln_g, lower_bounds, hgrn_norm_g, w_out, ffn_norm_g, w_gate, w_up, w_down, out):
    def scratch(name, shape):
        return nc.dram_tensor(name, shape, F32).ap()

    mid = {
        "qk_hi": scratch("qk_hi", (2 * W, SEQ)), "qk_lo": scratch("qk_lo", (2 * W, SEQ)),
        "v_hi": scratch("v_hi", (SEQ, W)), "v_lo": scratch("v_lo", (SEQ, W)),
        "hq": scratch("hq", (W, SEQ)), "hf": scratch("hf", (W, SEQ)), "hk": scratch("hk", (W, SEQ)),
        "hv": scratch("hv", (SEQ, W)), "hgate": scratch("hgate", (SEQ, W)),
    }
    mix = scratch("mix", (D, SEQ))
    with ExitStack() as ctx:
        a = Alloc(nc, ctx, "all")
        ident, ones = (a.sb(n, [P, P]) for n in ("ident", "ones"))
        pair_sel = a.sb("pair_sel", [P, 2])
        eps = a.sb("eps", [P, 1])
        make_constants(nc, ident, pair_sel, ones, eps)
        project(nc, x[0], attn_norm_g[0], w_in[0], q_norm_g[0], k_norm_g[0], ident, pair_sel, eps, mid)
        attend(nc, mid, (lambda_q1[0], lambda_k1[0], lambda_q2[0], lambda_k2[0]), subln_g[0], ident, eps, mix)
        recur(nc, mid, hgrn_norm_g[0], ident, eps, mix)
        feed(nc, x[0], mix, w_out[0], ffn_norm_g[0], w_gate[0], w_up[0], w_down[0], ident, ones, eps, out[0])


_INS = ['x', 'attn_norm_g', 'w_in', 'q_norm_g', 'k_norm_g', 'lambda_q1', 'lambda_k1', 'lambda_q2', 'lambda_k2',
        'subln_g', 'lower_bounds', 'hgrn_norm_g', 'w_out', 'ffn_norm_g', 'w_gate', 'w_up', 'w_down']
_OUTS = [((1, 2048, 1024), 'float32')]


def kernel(**inputs):
    import numpy as _np
    import concourse.bacc as _bacc
    from concourse import mybir as _mybir
    from concourse.bass_utils import run_bass_kernel_spmd as _run

    nc = _bacc.Bacc("TRN2", target_bir_lowering=False, num_devices=1)
    arrays, args = {}, []
    for name in _INS:
        a = _np.ascontiguousarray(inputs[name])
        arrays[f"in_{name}_dram"] = a
        args.append(nc.dram_tensor(f"in_{name}_dram", a.shape, _mybir.dt.from_np(a.dtype), kind="ExternalInput").ap())
    for i, (shape, dtype) in enumerate(_OUTS):
        dt = _mybir.dt.from_np(_np.dtype(dtype))
        args.append(nc.dram_tensor(f"out_{i}_dram", shape, dt, kind="ExternalOutput").ap())
    hybrid_trunk_kernel(nc, *args)
    r = _run(nc, [arrays], core_ids=[0])
    got = tuple(r.results[0][f"out_{i}_dram"] for i in range(len(_OUTS)))
    return got[0]
```

```python
from contextlib import ExitStack

import concourse.bass as bass
from concourse import mybir

P = 128
D = 1024
SEQ = 2048
DH = 64
HEADS = 4
W = 512
D_FF = 2816
EPS = 1e-6
LAM_INIT = 0.8 - 0.6

TB = 512
BLOCKS = SEQ // TB
SUB = TB // P
HGRN_LEVELS = P.bit_length() - 1
KS = D // P
UC = 256
UT = UC // P

F32 = mybir.dt.float32
F32R = mybir.dt.float32r

ALU = mybir.AluOpType
ACT = mybir.ActivationFunctionType
AX = mybir.AxisListType


class Count:

    def __init__(self, sem, credit=0):
        self.sem, self.credit = sem, credit

    def wait(self, eng, value):
        eng.wait_ge(self.sem, value + self.credit)


class Alloc:

    def __init__(self, nc, ctx, prefix):
        self.nc, self.ctx, self.prefix = nc, ctx, prefix

    def sb(self, name, shape, dt=F32):
        return self.ctx.enter_context(self.nc.sbuf_tensor(f"{self.prefix}_{name}", shape, dt))

    def bank(self, name):
        return self.ctx.enter_context(self.nc.psum_tensor(f"{self.prefix}_{name}", [P, 512], F32))

    def sem(self, name):
        return self.ctx.enter_context(self.nc.semaphore(f"{self.prefix}_{name}"))


def make_constants(nc, ident, pair_sel, ones, eps):
    with ExitStack() as ctx:
        a = Alloc(nc, ctx, "const")
        ident_zeroed = a.sem("ident_zeroed")
        pair_zeroed = a.sem("pair_zeroed")
        block = ctx.enter_context(nc.Block())

        @block.gpsimd
        def _(pool):
            nc.gpsimd.memset(ident[:], 0.0).then_inc(ident_zeroed, 1)
            pool.wait_ge(ident_zeroed, 1)
            nc.gpsimd.affine_select(out=ident[:], in_=ident[:], compare_op=ALU.not_equal, fill=1.0, base=0,
                                    pattern=[[-1, P]], channel_multiplier=1)

        @block.vector
        def _(dve):
            nc.vector.memset(pair_sel[:], 0.0).then_inc(pair_zeroed, 1)
            nc.vector.memset(ones[:], 1.0)
            nc.vector.memset(eps[:], EPS)
            dve.wait_ge(pair_zeroed, 1)
            for m in range(2):
                part = slice(m * DH, (m + 1) * DH)
                nc.vector.memset(pair_sel[part, m:m + 1], 1.0)


def make_level_masks(nc, pool, masks, work, made):
    width = masks.shape[2]
    chunks = width // (P // 2)
    steps = 0
    for m in range(masks.shape[1]):
        j = 1 << m
        if steps:
            pool.wait_ge(made, steps)
        nc.gpsimd.memset(work[:], 1.0).then_inc(made, 1)
        view = work[:].rearrange("p (a n j) -> p a n j", a=chunks, j=j)
        for base, sign, end in ((0, 1, 0), (j - 1, -1, 1)):
            pool.wait_ge(made, steps + end + 1)
            nc.gpsimd.affine_select(out=view, in_=view, compare_op=ALU.is_ge, fill=0.0, base=base,
                                    pattern=[[0, chunks], [-sign * 2 * j, P // (2 * j)], [0, j]],
                                    channel_multiplier=sign).then_inc(made, 1)
        pool.wait_ge(made, steps + 3)
        nc.gpsimd.tensor_copy(masks[:, m, :], work[:]).then_inc(made, 1)
        steps += 4


def project(nc, x, attn_g, w_in, q_g, k_g, ident, pair_sel, eps, out, masks):
    UNITS = w_in.shape[1] // UC
    PER_TURN = 2 * UNITS
    QK, V, HQ, HF, HI, HG = range(4), range(4, 6), range(6, 8), range(8, 10), range(10, 12), range(12, 14)
    TOKEN_MAJOR = (*V, *HI, *HG)
    SQUARES = {4: (0, 1), 5: (2, 3)}
    SCALE_STEP = 6
    SLABS = {7: (0, 1), 8: (2,), 9: (3,), 10: (4,), 11: (5,), 12: (6,), 13: (7,)}
    w_view = w_in.rearrange("(s p) n -> p s n", p=P)

    with ExitStack() as ctx:
        a = Alloc(nc, ctx, "proj")
        x_tok = a.sb("x_tok", [P, SUB, D])
        junk = a.sb("junk", [P, D])
        x_sumsq = a.sb("x_sumsq", [P, SUB])
        x_rms = a.sb("x_rms", [P, SUB])
        x_rrms = a.sb("x_rrms", [P, SUB])
        g_col = a.sb("g_col", [P, KS])
        qk_g = a.sb("qk_g", [P, 2])
        qk_gs = a.sb("qk_gs", [P, 2])
        h_hi = [a.sb(f"h_hi{b}", [P, KS, TB], F32R) for b in range(2)]
        h_lo = [a.sb(f"h_lo{b}", [P, KS, TB], F32R) for b in range(2)]
        w_raw = [a.sb(f"w_raw{b}", [P, KS, UC]) for b in range(2)]
        w_hi = [a.sb(f"w_hi{b}", [P, KS, UC], F32R) for b in range(2)]
        w_lo = [a.sb(f"w_lo{b}", [P, KS, UC], F32R) for b in range(2)]
        qk_raw = a.sb("qk_raw", [P, UT, TB])
        qk_sq = a.sb("qk_sq", [P, UT, TB])
        qk_rms = a.sb("qk_rms", [P, UT, SUB * 2])
        qk_rrms = a.sb("qk_rrms", [P, UT, SUB * 2])
        qk_spread = a.sb("qk_spread", [P, UT, SUB, P])
        stage = [[a.sb(f"stage{b}{k}", [P, UT, TB]) for k in range(2)] for b in range(2)]
        mask_work = a.sb("mask_work", [P, masks.shape[2]])
        prod = [[a.bank(f"prod{b}{t}") for t in range(UT)] for b in range(2)]
        turned = [a.bank(f"turned{b}") for b in range(2)]
        sums = [a.bank(f"sums{t}") for t in range(UT)]

        waited = a.sem("waited")
        mask_step = a.sem("mask_step")
        gains_in = a.sem("gains_in")
        gain_scaled = a.sem("gain_scaled")
        x_in = a.sem("x_in")
        w_in_sem = [a.sem(f"w_in{b}") for b in range(2)]
        w_hi_made = a.sem("w_hi_made")
        w_lo_made = a.sem("w_lo_made")
        unit_done = Count(a.sem("unit_done"), 1)
        squares_made = a.sem("squares_made")
        x_rms_made = a.sem("x_rms_made")
        x_rrms_made = a.sem("x_rrms_made")
        x_scaled = a.sem("x_scaled")
        slab_turned = a.sem("slab_turned")
        h_hi_made = a.sem("h_hi_made")
        h_lo_made = a.sem("h_lo_made")
        raw_made = a.sem("raw_made")
        sq_made = a.sem("sq_made")
        sums_made = a.sem("sums_made")
        rms_made = a.sem("rms_made")
        rrms_made = a.sem("rrms_made")
        widened = a.sem("widened")
        spread = a.sem("spread")
        norm_made = a.sem("norm_made")
        norm_hi_made = a.sem("norm_hi_made")
        act_part = a.sem("act_part")
        finished = [Count(a.sem(f"finished{b}"), 1) for b in range(2)]
        stored = [Count(a.sem(f"stored{b}"), 16) for b in range(2)]
        block = ctx.enter_context(nc.Block())

        def tokens_after(i, p):
            return (2 * i + 1) * TB if p == 0 else (1 - i) * 2 * TB

        def feature_dst(array, u0, u, tok):
            return array[(u - u0) * UC:(u - u0 + 1) * UC, bass.ds(tok, TB)].rearrange("(t p) n -> p t n", p=P)

        def token_dst(array, u0, u, tok):
            return array[bass.ds(tok, TB), (u - u0) * UC:(u - u0 + 1) * UC].rearrange("(t p) n -> p t n", p=P)

        def destinations(u, tok):
            if u in QK:
                return [feature_dst(out[k], 0, u, tok) for k in ("qk_hi", "qk_lo")]
            if u in V:
                return [token_dst(out[k], V[0], u, tok) for k in ("v_hi", "v_lo")]
            if u in HQ:
                return [feature_dst(out["hq"], HQ[0], u, tok)]
            if u in HF:
                return [feature_dst(out[k], HF[0], u, tok) for k in ("hf", "hk")]
            return [token_dst(out["hv"], HI[0], u, tok) if u in HI else token_dst(out["hgate"], HG[0], u, tok)]

        def stored_before(par, n):
            return sum(16 * len(destinations(m % UNITS, 0)) for m in range(n) if m % 2 == par)

        STORED_PER_TURN = [stored_before(par, PER_TURN) for par in range(2)]

        def staged_view(u, k, par):
            t = stage[par][k][:]
            if u in TOKEN_MAJOR:
                return t.rearrange("p t (b n) -> p (t b) n", b=2)
            return t

        @block.sync
        def _(sp):
            sp.dma_start(g_col[:], attn_g.rearrange("(s p) -> p s", p=P), allow_slow_non_contiguous=True).then_inc(gains_in, 16)
            for m in range(2):
                part = slice(m * DH, (m + 1) * DH)
                sp.dma_start(qk_g[part, 0:1], q_g.rearrange("(p o) -> p o", o=1)).then_inc(gains_in, 16)
                sp.dma_start(qk_g[part, 1:2], k_g.rearrange("(p o) -> p o", o=1)).then_inc(gains_in, 16)

            def load_x(tok):
                sp.dma_start(x_tok[:], x[bass.ds(tok, TB), :].rearrange("(t p) d -> p t d", p=P)).then_inc(x_in, 16)

            def load_w(u):
                u = u % UNITS
                sp.dma_start(w_raw[u % 2][:], w_view[:, :, u * UC:(u + 1) * UC]).then_inc(w_in_sem[u % 2], 16)

            def store(i, n):
                u = n % UNITS
                finished[u % 2].wait(sp, i * UNITS + n // 2 + 1)
                sp.sem_inc(waited, 1)
                for k, dst in enumerate(destinations(u, (2 * i + n // UNITS) * TB)):
                    sp.dma_start(dst, staged_view(u, k, u % 2)).then_inc(stored[u % 2].sem, 16)

            load_x(0)
            load_w(0)
            load_w(1)
            with sp.Fori(0, BLOCKS // 2) as i:
                for n in range(PER_TURN):
                    p, u = divmod(n, UNITS)
                    sp.wait_ge(w_lo_made, i * PER_TURN + n + 1)
                    load_w(n + 2)
                    if u == 1:
                        sp.wait_ge(slab_turned, (2 * i + p + 1) * KS)
                        sp.sem_inc(waited, 1)
                        load_x(tokens_after(i, p))
                    store(i, n)
            for par in range(2):
                stored[par].wait(sp, 2 * STORED_PER_TURN[par])
                sp.wait_ge(w_in_sem[par], 16 * (PER_TURN + 1))
            sp.wait_ge(x_in, 16 * (BLOCKS + 1))

        def earlier(par, i, n):
            return i * UNITS + (n + 1 - par) // 2

        HANDED = [(u, t) for u in (*V, *HQ, *HG) for t in range(UT)]

        def handed(i, n, t):
            p, u = divmod(n, UNITS)
            return (2 * i + p) * len(HANDED) + HANDED.index((u, t)) + 1

        @block.scalar
        def _(act):
            def split_w(i, n):
                par = n % 2
                act.wait_ge(w_in_sem[par], i * (16 * UNITS) + 16 * (n // 2 + 1))
                unit_done.wait(act, i * PER_TURN + (n - 1 if n else 0))
                nc.scalar.activation(w_hi[par][:], w_raw[par][:], ACT.Copy).then_inc(w_hi_made, 1)

            def square_x(nb, t):
                if t == 0:
                    act.wait_ge(x_in, (nb + 1) * 16)
                else:
                    act.wait_ge(squares_made, nb * SUB + t)
                nc.scalar.activation(junk[:], x_tok[:, t, :], ACT.Square, accum_out=x_sumsq[:, t:t + 1]).then_inc(squares_made, 1)
                if t == SUB - 1:
                    act.wait_ge(squares_made, (nb + 1) * SUB)
                    nc.scalar.activation(x_rms[:], x_sumsq[:], ACT.Sqrt, bias=eps[:], scale=1.0 / D).then_inc(x_rms_made, 1)

            def h_high(nb, s, buf):
                act.wait_ge(slab_turned, nb * KS + s + 1)
                nc.scalar.activation(h_hi[buf][:, s, :], turned[s % 2][:], ACT.Copy, scale=g_col[:, s:s + 1]).then_inc(h_hi_made, 1)

            def finish(i, n):
                p, u = divmod(n, UNITS)
                par = n % 2
                banks, (first, second) = prod[par], stage[par]
                unit_done.wait(act, i * PER_TURN + n + 1)
                if u in QK:
                    T = (2 * i + p) * (len(QK) * UT) + u * UT
                    finished[1 - par].wait(act, earlier(1 - par, i, n))
                    for t in range(UT):
                        nc.scalar.activation(qk_raw[:, t, :], banks[t][:], ACT.Copy).then_inc(raw_made, 1)
                    for t in range(UT):
                        act.wait_ge(raw_made, T + t + 1)
                        nc.scalar.activation(qk_sq[:, t, :], qk_raw[:, t, :], ACT.Square).then_inc(sq_made, 1)
                    for t in range(UT):
                        act.wait_ge(sums_made, T + t + 1)
                        nc.scalar.activation(qk_rms[:, t, :], sums[t][:, 0:SUB * 2], ACT.Sqrt, bias=eps[:], scale=1.0 / DH).then_inc(rms_made, 1)
                    return
                stored[par].wait(act, i * STORED_PER_TURN[par] + stored_before(par, n))
                for t in range(UT):
                    if u in V:
                        nc.scalar.activation(first[:, t, :].bitcast(F32R), banks[t][:], ACT.Copy).then_inc(act_part, 1)
                    elif u in HQ or u in HG:
                        nc.scalar.activation(second[:, t, :], banks[t][:], ACT.Sigmoid).then_inc(act_part, 1)
                    elif u in HI:
                        last = nc.scalar.activation(first[:, t, :], banks[t][:], ACT.Copy)
                    else:
                        nc.scalar.activation(first[:, t, :], banks[t][:], ACT.Sigmoid)
                        last = nc.scalar.activation(second[:, t, :], banks[t][:], ACT.Sigmoid, scale=-1.0)
                if u in HI or u in HF:
                    last.then_inc(finished[par].sem, 1)

            act.wait_ge(gains_in, 80)
            for t in range(SUB):
                square_x(0, t)
            for s in range(KS):
                h_high(0, s, 0)
            split_w(0, 0)
            with act.Fori(0, BLOCKS // 2) as i:
                for n in range(PER_TURN):
                    p, u = divmod(n, UNITS)
                    nb = 2 * i + p + 1
                    split_w(i, n + 1)
                    for t in SQUARES.get(u, ()):
                        square_x(nb, t)
                    for s in SLABS.get(u, ()):
                        h_high(nb, s, 1 - p)
                    finish(i, n)

        @block.gpsimd
        def _(pool):
            make_level_masks(nc, pool, masks, mask_work, mask_step)

        @block.vector
        def _(dve):
            def split_w(i, n):
                par = n % 2
                dve.wait_ge(w_hi_made, i * PER_TURN + n + 1)
                nc.vector.tensor_tensor(w_lo[par][:], w_raw[par][:], w_hi[par][:].bitcast(F32), ALU.subtract).then_inc(w_lo_made, 1)

            def scale_x(nb):
                dve.wait_ge(x_rms_made, nb + 1)
                nc.vector.reciprocal(x_rrms[:], x_rms[:]).then_inc(x_rrms_made, 1)
                dve.wait_ge(x_rrms_made, nb + 1)
                for t in range(SUB):
                    nc.vector.tensor_scalar(x_tok[:, t, :], x_tok[:, t, :], x_rrms[:, t:t + 1], None, ALU.mult).then_inc(x_scaled, 1)

            def h_low(nb, s, buf):
                dve.wait_ge(h_hi_made, nb * KS + s + 1)
                nc.vector.scalar_tensor_tensor(out=h_lo[buf][:, s, :], in0=turned[s % 2][:], scalar=g_col[:, s:s + 1],
                                               in1=h_hi[buf][:, s, :].bitcast(F32), op0=ALU.mult,
                                               op1=ALU.subtract).then_inc(h_lo_made, 1)

            def finish(i, n):
                p, u = divmod(n, UNITS)
                par = n % 2
                banks, (first, second) = prod[par], stage[par]
                if u in QK:
                    T = (2 * i + p) * (len(QK) * UT) + u * UT
                    gain = (qk_gs[:, 0:1], qk_gs[:, 1:2])[u * UC // W]
                    stored[par].wait(dve, i * STORED_PER_TURN[par] + stored_before(par, n))
                    for t in range(UT):
                        dve.wait_ge(rms_made, T + t + 1)
                        nc.vector.reciprocal(qk_rrms[:, t, :], qk_rms[:, t, :]).then_inc(rrms_made, 1)
                        dve.wait_ge(rrms_made, T + t + 1)
                        wide = qk_spread[:, t].rearrange("p b (m f) -> p (b m) f", m=2)
                        nc.vector.tensor_copy(wide, qk_rrms[:, t, :].unsqueeze(2).to_broadcast([P, SUB * 2, DH])).then_inc(widened, 1)
                    for t in range(UT):
                        dve.wait_ge(spread, T + t + 1)
                        nc.vector.scalar_tensor_tensor(out=qk_raw[:, t, :], in0=qk_raw[:, t, :], scalar=gain,
                                                       in1=banks[t][:], op0=ALU.mult, op1=ALU.mult).then_inc(norm_made, 1)
                        dve.wait_ge(norm_made, T + t + 1)
                        nc.vector.tensor_copy(first[:, t, :].bitcast(F32R), qk_raw[:, t, :]).then_inc(norm_hi_made, 1)
                        dve.wait_ge(norm_hi_made, T + t + 1)
                        last = nc.vector.tensor_tensor(second[:, t, :].bitcast(F32R), qk_raw[:, t, :], first[:, t, :], ALU.subtract)
                elif u in V:
                    for t in range(UT):
                        dve.wait_ge(act_part, handed(i, n, t))
                        last = nc.vector.tensor_tensor(second[:, t, :].bitcast(F32R), banks[t][:], first[:, t, :], ALU.subtract)
                elif u in HQ or u in HG:
                    for t in range(UT):
                        dve.wait_ge(act_part, handed(i, n, t))
                        last = nc.vector.tensor_tensor(first[:, t, :], banks[t][:], second[:, t, :], ALU.mult)
                else:
                    return
                last.then_inc(finished[par].sem, 1)

            for count in (unit_done, *finished, *stored):
                dve.sem_inc(count.sem, count.credit)
            dve.wait_ge(gains_in, 80)
            nc.vector.tensor_scalar(qk_gs[:, 0:1], qk_g[:, 0:1], DH ** -0.5, None, ALU.mult).then_inc(gain_scaled, 1)
            nc.vector.tensor_copy(qk_gs[:, 1:2], qk_g[:, 1:2]).then_inc(gain_scaled, 1)
            dve.wait_ge(gain_scaled, 2)
            scale_x(0)
            for s in range(KS):
                h_low(0, s, 0)
            split_w(0, 0)
            with dve.Fori(0, BLOCKS // 2) as i:
                for n in range(PER_TURN):
                    p, u = divmod(n, UNITS)
                    nb = 2 * i + p + 1
                    split_w(i, n + 1)
                    if u == SCALE_STEP:
                        scale_x(nb)
                    for s in SLABS.get(u, ()):
                        h_low(nb, s, 1 - p)
                    finish(i, n)

        @block.tensor
        def _(pe):
            def turn_slab(nb, s, first_block=False):
                pe.wait_ge(x_scaled, (nb + 1) * SUB)
                if not (first_block and s < 2):
                    pe.wait_ge(h_lo_made, nb * KS + s - 1)
                for t in range(SUB):
                    last = pe.transpose(turned[s % 2][:, t * P:(t + 1) * P], x_tok[:, t, s * P:(s + 1) * P], ident[:])
                last.then_inc(slab_turned, 1)

            def sum_squares(i, n):
                p, u = divmod(n, UNITS)
                T = (2 * i + p) * (len(QK) * UT) + u * UT
                for t in range(UT):
                    pe.wait_ge(sq_made, T + t + 1)
                    for b in range(SUB):
                        last = pe.matmul(sums[t][:, 2 * b:2 * b + 2], qk_sq[:, t, b * P:(b + 1) * P], pair_sel[:],
                                         start=True, stop=True)
                    last.then_inc(sums_made, 1)

            def spread_scales(i, n):
                p, u = divmod(n, UNITS)
                T = (2 * i + p) * (len(QK) * UT) + u * UT
                for t in range(UT):
                    pe.wait_ge(widened, T + t + 1)
                    for b in range(SUB):
                        last = pe.matmul(prod[n % 2][t][:, b * P:(b + 1) * P], qk_spread[:, t, b, :], ident[:],
                                         start=True, stop=True)
                    last.then_inc(spread, 1)

            for s in range(KS):
                turn_slab(0, s, True)
            pe.wait_ge(h_lo_made, KS)
            with pe.Fori(0, BLOCKS // 2) as i:
                for n in range(PER_TURN):
                    p, u = divmod(n, UNITS)
                    par = n % 2
                    nb = 2 * i + p + 1
                    hi, lo, wh, wl = h_hi[p], h_lo[p], w_hi[par], w_lo[par]
                    if u == 0:
                        pe.wait_ge(h_lo_made, nb * KS)
                    pe.wait_ge(w_lo_made, i * PER_TURN + n + 1)
                    finished[par].wait(pe, i * UNITS + n // 2)

                    def other_work(quarter):
                        if u and u - 1 in QK:
                            if quarter == 1:
                                sum_squares(i, n - 1)
                            elif quarter == 2:
                                spread_scales(i, n - 1)
                        elif quarter == 1:
                            for s in SLABS.get(u, ()):
                                turn_slab(nb, s)

                    if u in TOKEN_MAJOR:
                        for t in range(SUB):
                            dst = prod[par][t // 2][:, (t % 2) * UC:(t % 2 + 1) * UC]
                            tok = slice(t * P, (t + 1) * P)
                            for s in range(KS):
                                pe.matmul(dst, hi[:, s, tok], wh[:, s, :], start=s == 0, stop=False)
                                pe.matmul(dst, hi[:, s, tok], wl[:, s, :], start=False, stop=False)
                                last = pe.matmul(dst, lo[:, s, tok], wh[:, s, :], start=False, stop=s == KS - 1)
                            if t < 2:
                                other_work(t + 1)
                    else:
                        for t in range(UT):
                            dst = prod[par][t][:]
                            col = slice(t * P, (t + 1) * P)
                            for s in range(KS):
                                pe.matmul(dst, wh[:, s, col], hi[:, s, :], start=s == 0, stop=False)
                                pe.matmul(dst, wh[:, s, col], lo[:, s, :], start=False, stop=False)
                                last = pe.matmul(dst, wl[:, s, col], hi[:, s, :], start=False, stop=s == KS - 1)
                                if t == 0 and s % (KS // 2) == KS // 2 - 1:
                                    other_work(1 + s // (KS // 2))
                    last.then_inc(unit_done.sem, 1)


def mix_tokens(nc, mid, lambdas, subln_g, hgrn_g, ident, eps, mask, mix):
    C = P
    LEVELS = HGRN_LEVELS
    CH = TB // C
    HALF = HEADS // 2
    HC = HALF * CH
    RUN = C // 2
    UPDATES = LEVELS + 1
    FILLS = ([("diagonal", h, n) for h in range(2) for n in range(HALF)]
             + [("level", h, m) for m in range(LEVELS) for h in range(2)]
             + [("k", c // 2, c) for c in range(CH)]
             + [(kind, 0, c) for c in range(CH) for kind in ("output", "state")])
    GATE_STEP = len(FILLS) // 2
    assert HEADS == BLOCKS and GATE_STEP < SEQ // P
    STEPS = SEQ // P
    RING = 4
    RUN_BANKS = 2
    GROUP = 512 // P
    MASKED = -1e30

    def banks_of(j):
        return j // GROUP + 1

    runs, at = {}, 0
    for j in range(STEPS):
        for m in range(2):
            runs[j, m], key, left = [], 0, (j + 1) * P
            while left:
                n = min(RING - at, RUN_BANKS, -(-left // 512))
                width = min(left, n * 512)
                runs[j, m].append((at, key, width))
                at, key, left = (at + n) % RING, key + width, left - width
    assert at == 0
    order = [(j, m, r) for j in range(STEPS) for m in range(2) for r in range(len(runs[j, m]))]
    RUNS = len(order)
    MAX_RUNS = max(len(rs) for rs in runs.values())
    RUN_AT = {key: n for n, key in enumerate(order)}
    freed, last_in = {}, {}
    for n, (j, m, r) in enumerate(order):
        bank, _, width = runs[j, m][r]
        mine = range(bank, bank + -(-width // 512))
        freed[j, m, r] = max([last_in.get(x, -1) for x in mine]) + 1
        last_in.update({x: n for x in mine})
    GROUPS = sum(banks_of(j) for j in range(STEPS))
    GROUP_AT = {(j, g): sum(banks_of(i) for i in range(j)) + g for j in range(STEPS) for g in range(banks_of(j))}
    assert GROUPS % 2 == 0

    def tiles_in(j, g):
        return min(GROUP, j + 1 - g * GROUP)

    with ExitStack() as ctx:
        a = Alloc(nc, ctx, "att")
        q_hl = [a.sb(f"q_hl{b}", [P, 2, TB], F32R) for b in range(2)]
        q_lh = [a.sb(f"q_lh{b}", [P, 2, TB], F32R) for b in range(2)]
        k_hl = a.sb("k_hl", [P, 2, SEQ], F32R)
        v_hi = a.sb("v_hi", [P, STEPS, P], F32R)
        v_lo = a.sb("v_lo", [P, STEPS, P], F32R)
        early = a.sb("early", [P, P], F32R)
        late = a.sb("late", [P, P], F32R)
        lams = a.sb("lams", [P, 4, DH])
        lam_dots = a.sb("lam_dots", [P, 2])
        lam_exps = a.sb("lam_exps", [P, 2])
        neg_lam = a.sb("neg_lam", [P, 1])
        g_col = a.sb("g_col", [P, 1])
        expo = [a.sb(f"expo{b}", [P, 2, SEQ]) for b in range(2)]
        neg_max = a.sb("neg_max", [P, 2, 2])
        run_neg_max = a.sb("run_neg_max", [P, 2, 2, MAX_RUNS])
        row_sum = a.sb("row_sum", [P, 2, 2, MAX_RUNS])
        total = a.sb("total", [P, 2, 2])
        inv = a.sb("inv", [P, 2, 2])
        ratio = a.sb("ratio", [P, 2])
        wt_hi = [a.sb(f"wt_hi{b}", [P, 512], F32R) for b in range(2)]
        wt_lo = [a.sb(f"wt_lo{b}", [P, 512], F32R) for b in range(2)]
        o_all = a.sb("o_all", [P, STEPS, P])
        o_sq = a.sb("o_sq", [P, P])
        o_sumsq = a.sb("o_sumsq", [P, STEPS])
        o_rms = a.sb("o_rms", [P, STEPS])
        o_rrms = a.sb("o_rrms", [P, STEPS])
        o_turned = a.sb("o_turned", [P, SEQ])
        ring = ctx.enter_context(nc.psum_tensor("att_ring", [P, RING * 512], F32))
        turned = [a.bank(f"turned{b}") for b in range(2)]
        out_bank = a.bank("out")

        r = Alloc(nc, ctx, "rec")
        rq, rk, rf = (r.sb(n, [P, HEADS, TB]) for n in ("q", "k", "f"))
        rv, rgate = (r.sb(n, [P, CH, W]) for n in ("v", "gate"))
        whole = [None] + [r.sb(f"whole{m}", [P, HEADS * TB >> m]) for m in range(1, LEVELS + 1)]
        rscore = r.sb("score", [P, HEADS, CH, C])
        k_tok = r.sb("k_tok", [P, CH, HEADS, C])
        state = r.sb("state", [P, HEADS, C])
        ro = r.sb("o", [P, CH, W])
        ro_sq = r.sb("o_sq", [P, W])
        ro_sumsq = r.sb("o_sumsq", [P, CH, HEADS])
        ro_rms = r.sb("o_rms", [P, CH * HEADS])
        ro_rrms = r.sb("o_rrms", [P, CH * HEADS])
        rg_col = r.sb("g_col", [P, 1])
        ro_turned = r.sb("o_turned", [P, HEADS, TB])
        fill_bank = r.bank("fill")

        waited = a.sem("waited")
        small_in = a.sem("small_in")
        chain = a.sem("chain")
        lam_exp_made = a.sem("lam_exp_made")
        q_in = [a.sem(f"q_in{b}") for b in range(2)]
        k_in = [a.sem(f"k_in{b}") for b in range(2)]
        v_in = [a.sem(f"v_in{b}") for b in range(2)]
        masks_made = a.sem("masks_made")
        scored = a.sem("scored")
        run_max = a.sem("run_max")
        max_made = a.sem("max_made")
        exp_made = a.sem("exp_made")
        total_made = a.sem("total_made")
        inv_made = a.sem("inv_made")
        ratio_made = a.sem("ratio_made")
        combined = a.sem("combined")
        group_turned = a.sem("group_turned")
        group_hi = a.sem("group_hi")
        group_lo = a.sem("group_lo")
        group_used = a.sem("group_used")
        o_read = a.sem("o_read")
        o_squared = a.sem("o_squared")
        o_rms_made = a.sem("o_rms_made")
        o_rrms_made = a.sem("o_rrms_made")
        o_normed = a.sem("o_normed")
        o_turn_done = a.sem("o_turn_done")
        o_staged = a.sem("o_staged")
        o_stored = Count(a.sem("o_stored"), 16)
        r_in = r.sem("in")
        rt_in = r.sem("tokens_in")
        whole_made = r.sem("whole_made")
        fill_done = r.sem("fill_done")
        fill_read = Count(r.sem("fill_read"), 1)
        q_ready = [r.sem(f"q_ready{h}") for h in range(2)]
        k_ready = [r.sem(f"k_ready{h}") for h in range(2)]
        state_made = Count(r.sem("state_made"), 1)
        r_squared = r.sem("squared")
        r_summed = Count(r.sem("summed"), 1)
        r_gated = r.sem("gated")
        r_rms_made = r.sem("rms_made")
        r_rrms_made = r.sem("rrms_made")
        r_scaled = r.sem("scaled")
        block = ctx.enter_context(nc.Block())
        R_DMAS = 3
        RT_DMAS = 2
        TURNS = SEQ // 512

        def filled(h, n):
            return h * len(FILLS) + n + 1

        def fill_at(*key):
            return FILLS.index(key)

        def half(t, side):
            return t[:, side * HALF:(side + 1) * HALF, :].rearrange("p h n -> p (h n)")

        def runs_of(t, side, m, right):
            return half(t, side).rearrange("p (n s j) -> p n s j", s=2, j=1 << m)[:, :, right, :]

        def factor(side, m, right):
            pairs = HC * (C >> m + 1)
            src = whole[m][:, side * 2 * pairs:(side + 1) * 2 * pairs] if m else half(rf, side)
            return src.rearrange("p (n s) -> p n s", s=2)[:, :, 1 - right].unsqueeze(2).to_broadcast([P, pairs, 1 << m])

        @block.sync
        def _(sp):
            low, high = slice(0, DH), slice(DH, P)

            def rows(name, h, base, tokens):
                return mid[name][bass.ds(h * P + base, P), tokens].rearrange("(m p) n -> p m n", p=DH)

            def load_q(h, g):
                tokens = slice(g * TB, (g + 1) * TB)
                for tile, names in ((q_hl, ("qk_hi", "qk_lo")), (q_lh, ("qk_lo", "qk_hi"))):
                    for part, name in zip((low, high), names):
                        sp.dma_start(tile[g % 2][part].bitcast(F32), rows(name, h, 0, tokens)).then_inc(q_in[g % 2], 16)

            def load_k(h, n):
                tokens = (slice(0, TB), slice(TB, SEQ))[n]
                for part, name in ((low, "qk_hi"), (high, "qk_lo")):
                    sp.dma_start(k_hl[part, :, tokens].bitcast(F32), rows(name, h, W, tokens)).then_inc(k_in[n], 16)

            def load_v(h, n):
                tiles = (slice(0, GROUP), slice(GROUP, STEPS))[n]
                for name, tile in (("v_hi", v_hi), ("v_lo", v_lo)):
                    src = mid[name][:, bass.ds(h * P, P)].rearrange("(t p) n -> p t n", p=P)[:, tiles, :]
                    sp.dma_start(tile[:, tiles, :].bitcast(F32), src).then_inc(v_in[n], 16)

            def load_features(tile, name, tok):
                sp.dma_start(tile[:], mid[name][:, bass.ds(tok, TB)].rearrange("(h p) n -> p h n", p=P)).then_inc(r_in, 16)

            def load_tokens(tile, name, tok):
                sp.dma_start(tile[:], mid[name][bass.ds(tok, TB), :].rearrange("(c p) n -> p c n", p=P)).then_inc(rt_in, 16)

            def step_scored(h, j):
                sp.wait_ge(scored, h * RUNS + RUN_AT[j, 1, len(runs[j, 1]) - 1] + 1)
                sp.sem_inc(waited, 1)

            def all_filled(h, n):
                sp.wait_ge(fill_done, filled(h, n))
                sp.sem_inc(waited, 1)

            load_k(0, 0)
            load_q(0, 0)
            for n, vec in enumerate(lambdas):
                sp.dma_start(lams[:, n, :], vec.partition_broadcast(P)).then_inc(small_in, 16)
            sp.dma_start(g_col[:], subln_g.rearrange("(p o) -> p o", o=1)).then_inc(small_in, 16)
            sp.dma_start(rg_col[:], hgrn_g.rearrange("(p o) -> p o", o=1)).then_inc(small_in, 16)
            load_features(rq, "hq", 0)
            load_features(rk, "hk", 0)
            load_features(rf, "hf", 0)
            load_v(0, 0)
            load_k(0, 1)
            load_q(0, 1)
            load_v(0, 1)
            load_tokens(rv, "hv", 0)
            load_tokens(rgate, "hgate", 0)
            with sp.Fori(0, HEADS) as h:
                after = (h + 1) % HEADS
                sp.wait_ge(q_ready[1], h * UPDATES + 2)
                sp.wait_ge(k_ready[1], h * LEVELS + 1)
                sp.sem_inc(waited, 1)
                load_features(rf, "hf", after * TB)
                step_scored(h, GROUP - 1)
                load_q(h, 2)
                step_scored(h, 2 * GROUP - 1)
                load_q(h, 3)
                all_filled(h, fill_at("k", 1, CH - 1))
                load_features(rk, "hk", after * TB)
                step_scored(h, 3 * GROUP - 1)
                load_q(after, 0)
                all_filled(h, len(FILLS) - 1)
                load_features(rq, "hq", after * TB)
                load_tokens(rv, "hv", after * TB)
                step_scored(h, STEPS - 1)
                load_k(after, 0)
                load_k(after, 1)
                load_q(after, 1)
                sp.wait_ge(group_used, h * GROUPS + GROUPS)
                sp.sem_inc(waited, 1)
                load_v(after, 0)
                load_v(after, 1)
                sp.wait_ge(r_gated, h + 1)
                sp.sem_inc(waited, 1)
                load_tokens(rgate, "hgate", after * TB)
                for c in range(TURNS):
                    sp.wait_ge(o_staged, h * (2 * TURNS) + c + 1)
                    sp.sem_inc(waited, 1)
                    sp.dma_start(mix[bass.ds(h * P, P), c * 512:(c + 1) * 512], o_turned[:, c * 512:(c + 1) * 512]).then_inc(o_stored.sem, 16)
                sp.wait_ge(o_staged, (h + 1) * (2 * TURNS))
                sp.sem_inc(waited, 1)
                sp.dma_start(mix[W:2 * W, bass.ds(h * TB, TB)].rearrange("(h p) n -> p h n", p=P), ro_turned[:]).then_inc(o_stored.sem, 16)
            o_stored.wait(sp, 16 * HEADS * (TURNS + 1))
            for n in range(2):
                sp.wait_ge(q_in[n], 64 * (2 * HEADS + 1))
                sp.wait_ge(k_in[n], 32 * (HEADS + 1))
                sp.wait_ge(v_in[n], 32 * (HEADS + 1))
            sp.wait_ge(r_in, 16 * R_DMAS * (HEADS + 1))
            sp.wait_ge(rt_in, 16 * RT_DMAS * (HEADS + 1))

        @block.gpsimd
        def _(pool):
            with pool.Fori(0, HEADS) as h:
                pool.wait_ge(r_in, h * (16 * R_DMAS) + 16 * R_DMAS)
                for m in range(LEVELS):
                    src = whole[m][:] if m else rf[:].rearrange("p h n -> p (h n)")
                    src = src.rearrange("p (n s) -> p n s", s=2)
                    if m:
                        pool.wait_ge(whole_made, h * LEVELS + m)
                    nc.gpsimd.tensor_tensor(whole[m + 1][:], src[:, :, 0], src[:, :, 1], ALU.mult).then_inc(whole_made, 1)
                for m in range(LEVELS):
                    for side in range(2):
                        pool.wait_ge(fill_done, filled(h, fill_at("level", side, m)))
                        if m:
                            pool.wait_ge(k_ready[side], h * LEVELS + m)
                        pool.sem_inc(waited, 1)
                        nc.gpsimd.tensor_tensor(runs_of(rk, side, m, 0), runs_of(rk, side, m, 0), factor(side, m, 0), ALU.mult).then_inc(k_ready[side], 1)
                pool.wait_ge(rt_in, h * (16 * RT_DMAS) + 16 * RT_DMAS)
                fill_read.wait(pool, filled(h, len(FILLS) - 1))
                nc.gpsimd.tensor_tensor(ro[:], ro[:], rgate[:], ALU.mult).then_inc(r_gated, 1)

        @block.scalar
        def _(act):
            def exponentiate(h, j, m):
                for r, (bank, key, width) in enumerate(runs[j, m]):
                    act.wait_ge(max_made, h * (2 * STEPS) + 2 * j + m + 1)
                    nc.scalar.activation(expo[j % 2][:, m, key:key + width], ring[:, bank * 512:bank * 512 + width], ACT.Exp,
                                         bias=neg_max[:, j % 2, m:m + 1],
                                         accum_out=row_sum[:, j % 2, m, r:r + 1]).then_inc(exp_made, 1)

            def group_high(h, j, g):
                k, n = GROUP_AT[j, g], tiles_in(j, g) * P
                act.wait_ge(group_turned, h * GROUPS + k + 1)
                if k >= 2:
                    act.wait_ge(group_used, h * GROUPS + k - 1)
                nc.scalar.activation(wt_hi[k % 2][:, 0:n], turned[k % 2][:, 0:n], ACT.Copy).then_inc(group_hi, 1)

            def read_output(h, j):
                act.wait_ge(group_used, h * GROUPS + GROUP_AT[j, banks_of(j) - 1] + 1)
                nc.scalar.activation(o_all[:, j, :], out_bank[:, 0:P], ACT.Copy, scale=inv[:, j % 2, 0:1]).then_inc(o_read, 1)
                act.wait_ge(o_read, h * STEPS + j + 1)
                if j:
                    act.wait_ge(o_squared, h * STEPS + j)
                nc.scalar.activation(o_sq[:], o_all[:, j, :], ACT.Square, accum_out=o_sumsq[:, j:j + 1]).then_inc(o_squared, 1)

            def read_fill(h, n):
                kind, _, c = FILLS[n]
                if kind not in ("k", "output"):
                    return
                act.wait_ge(fill_done, filled(h, n))
                if kind == "k":
                    nc.scalar.activation(k_tok[:, c].rearrange("p h n -> p (h n)"), fill_bank[:], ACT.Copy).then_inc(fill_read.sem, 1)
                    return
                r_summed.wait(act, h * CH + c)
                nc.scalar.activation(ro_sq[:], fill_bank[:], ACT.Square).then_inc(r_squared, 1)
                act.wait_ge(r_squared, h * CH + c + 1)
                nc.scalar.activation(ro[:, c], fill_bank[:], ACT.Copy).then_inc(fill_read.sem, 1)

            act.wait_ge(chain, 2)
            nc.scalar.activation(lam_exps[:], lam_dots[:], ACT.Exp).then_inc(lam_exp_made, 1)
            with act.Fori(0, HEADS) as h:
                for j in range(STEPS + 1):
                    groups = range(banks_of(j - 1)) if j else ()
                    if j < STEPS:
                        exponentiate(h, j, 0)
                    if j >= 2:
                        read_output(h, j - 2)
                    if j < GATE_STEP:
                        read_fill(h, 2 * j)
                    for g in groups[:2]:
                        group_high(h, j - 1, g)
                    if j < STEPS:
                        exponentiate(h, j, 1)
                    if j < GATE_STEP:
                        read_fill(h, 2 * j + 1)
                    for g in groups[2:]:
                        group_high(h, j - 1, g)
                act.wait_ge(r_summed.sem, h * CH + CH + r_summed.credit)
                nc.scalar.activation(ro_rms[:], ro_sumsq[:].rearrange("p c h -> p (c h)"), ACT.Sqrt, bias=eps[:], scale=1.0 / C).then_inc(r_rms_made, 1)
                read_output(h, STEPS - 1)
                act.wait_ge(o_squared, h * STEPS + STEPS)
                nc.scalar.activation(o_rms[:], o_sumsq[:], ACT.Sqrt, bias=eps[:], scale=1.0 / P).then_inc(o_rms_made, 1)
                o_stored.wait(act, h * (16 * (TURNS + 1)))
                for c in range(2 * TURNS):
                    act.wait_ge(o_turn_done, h * (2 * TURNS) + c + 1)
                    if c < TURNS:
                        nc.scalar.activation(o_turned[:, c * 512:(c + 1) * 512], turned[c % 2][:], ACT.Copy, scale=g_col[:]).then_inc(o_staged, 1)
                    else:
                        nc.scalar.activation(ro_turned[:, c - TURNS, :], turned[c % 2][:], ACT.Copy, scale=rg_col[:]).then_inc(o_staged, 1)

        @block.vector
        def _(dve):
            def maximum(h, j, m):
                n_runs, final = len(runs[j, m]), neg_max[:, j % 2, m:m + 1]
                for r, (bank, key, width) in enumerate(runs[j, m]):
                    dve.wait_ge(scored, h * RUNS + RUN_AT[j, m, r] + 1)
                    dst = run_neg_max[:, j % 2, m, r:r + 1] if n_runs > 1 else final
                    last = nc.vector.tensor_reduce(dst, ring[:, bank * 512:bank * 512 + width], AX.X, ALU.max, negate=True)
                    if n_runs > 1:
                        last.then_inc(run_max, 1)
                if n_runs > 1:
                    dve.wait_ge(run_max, h * SPLIT_RUNS + split_runs(j, m))
                    last = nc.vector.tensor_reduce(final, run_neg_max[:, j % 2, m, 0:n_runs], AX.X, ALU.min)
                last.then_inc(max_made, 1)

            def split_runs(j, m):
                return sum(len(runs[key]) for key in runs if key <= (j, m) and len(runs[key]) > 1)

            SPLIT_RUNS = split_runs(STEPS, 0)

            def combine(h, j):
                b = j % 2
                dve.wait_ge(exp_made, h * RUNS + RUN_AT[j, 1, len(runs[j, 1]) - 1] + 1)
                n_runs = [len(runs[j, m]) for m in range(2)]
                for m in range(2):
                    last = nc.vector.tensor_reduce(total[:, b, m:m + 1], row_sum[:, b, m, 0:n_runs[m]], AX.X, ALU.add)
                    last.then_inc(total_made, 1)
                dve.wait_ge(total_made, (h * STEPS + j + 1) * 2)
                nc.vector.reciprocal(inv[:, b, :], total[:, b, :]).then_inc(inv_made, 1)
                dve.wait_ge(inv_made, h * STEPS + j + 1)
                nc.vector.scalar_tensor_tensor(out=ratio[:, b:b + 1], in0=total[:, b, 0:1], scalar=neg_lam[:],
                                               in1=inv[:, b, 1:2], op0=ALU.mult, op1=ALU.mult).then_inc(ratio_made, 1)
                dve.wait_ge(ratio_made, h * STEPS + j + 1)
                n = (j + 1) * P
                nc.vector.scalar_tensor_tensor(out=expo[b][:, 0, 0:n], in0=expo[b][:, 1, 0:n], scalar=ratio[:, b:b + 1],
                                               in1=expo[b][:, 0, 0:n], op0=ALU.mult, op1=ALU.add).then_inc(combined, 1)

            def group_low(h, j, g):
                k, n = GROUP_AT[j, g], tiles_in(j, g) * P
                dve.wait_ge(group_hi, h * GROUPS + k + 1)
                nc.vector.tensor_tensor(wt_lo[k % 2][:, 0:n], turned[k % 2][:, 0:n], wt_hi[k % 2][:, 0:n].bitcast(F32), ALU.subtract).then_inc(group_lo, 1)

            def raise_level(h, side, m):
                if m:
                    dve.wait_ge(whole_made, h * LEVELS + m)
                dve.wait_ge(q_ready[side], h * UPDATES + m + 1)
                nc.vector.tensor_tensor(runs_of(rq, side, m, 1), runs_of(rq, side, m, 1), factor(side, m, 1), ALU.mult).then_inc(q_ready[side], 1)

            def read_fill(h, n):
                kind, side, at = FILLS[n]
                if kind in ("k", "output"):
                    return
                dve.wait_ge(fill_done, filled(h, n))
                dve.sem_inc(waited, 1)
                if kind == "diagonal":
                    nc.vector.tensor_tensor(rscore[:, side * HALF + at], fill_bank[:].rearrange("p (c t) -> p c t", t=C),
                                            ident[:].unsqueeze(1).to_broadcast([P, CH, C]), ALU.mult).then_inc(fill_read.sem, 1)
                    if at == HALF - 1:
                        nc.vector.tensor_tensor(half(rq, side), half(rq, side), half(rf, side), ALU.mult).then_inc(q_ready[side], 1)
                elif kind == "level":
                    raise_level(h, side, at)
                    fill_read.wait(dve, filled(h, n) - 1)
                    dve.sem_inc(waited, 1)
                    dst = rscore[:, side * HALF:(side + 1) * HALF].rearrange("p h c (n s j) -> p (h c n) s j", s=2, j=1 << at)[:, :, 1, :]
                    nc.vector.copy_predicated(dst, mask[:, at].rearrange("p (n j) -> p n j", j=1 << at),
                                              fill_bank[:].rearrange("p (n j) -> p n j", j=1 << at)).then_inc(fill_read.sem, 1)
                else:
                    state_made.wait(dve, (h * CH + at) * (HEADS - 1))
                    for hh in range(HEADS):
                        last = nc.vector.scalar_tensor_tensor(out=state[:, hh, :], in0=state[:, hh, :],
                                                              scalar=whole[LEVELS][:, hh * CH + at:hh * CH + at + 1],
                                                              in1=fill_bank[:, hh * C:(hh + 1) * C], op0=ALU.mult, op1=ALU.add)
                        last.then_inc(state_made.sem if hh < HEADS - 1 else fill_read.sem, 1)
                    dve.wait_ge(r_squared, h * CH + at + 1)
                    nc.vector.tensor_reduce(ro_sumsq[:, at], ro_sq[:].rearrange("p (h n) -> p h n", n=C), AX.X, ALU.add).then_inc(r_summed.sem, 1)

            for count in (o_stored, fill_read, state_made, r_summed):
                dve.sem_inc(count.sem, count.credit)
            nc.vector.memset(state[:], 0.0)
            nc.vector.memset(early[:].bitcast(F32), 0.0).then_inc(masks_made, 1)
            nc.vector.memset(late[:].bitcast(F32), 0.0).then_inc(masks_made, 1)
            dve.wait_ge(masks_made, 2)
            nc.vector.memset(early[0:1, 0:P // 2].bitcast(F32), 1.0).then_inc(masks_made, 1)
            nc.vector.memset(late[0:1, P // 2:P].bitcast(F32), MASKED).then_inc(masks_made, 1)
            dve.wait_ge(small_in, 16 * 6)
            for n in range(2):
                nc.vector.tensor_tensor_reduce(out=lams[:, 2 * n, :], in0=lams[:, 2 * n, :], in1=lams[:, 2 * n + 1, :], scale=1.0,
                                               scalar=0.0, op0=ALU.mult, op1=ALU.add, accum_out=lam_dots[:, n:n + 1]).then_inc(chain, 1)
            nc.vector.tensor_scalar(g_col[:], g_col[:], 1.0 - LAM_INIT, None, ALU.mult).then_inc(chain, 1)
            dve.wait_ge(lam_exp_made, 1)
            nc.vector.tensor_tensor(neg_lam[:], lam_exps[:, 1:2], lam_exps[:, 0:1], ALU.subtract).then_inc(chain, 1)
            dve.wait_ge(chain, 4)
            nc.vector.tensor_scalar(neg_lam[:], neg_lam[:], -LAM_INIT, None, ALU.add).then_inc(chain, 1)
            dve.wait_ge(chain, 5)
            with dve.Fori(0, HEADS) as h:
                for j in range(STEPS + 1):
                    groups = range(banks_of(j - 1)) if j else ()
                    if j:
                        combine(h, j - 1)
                    if j < STEPS:
                        maximum(h, j, 0)
                    if j == 0:
                        dve.wait_ge(r_in, h * (16 * R_DMAS) + 16 * R_DMAS)
                    if j < GATE_STEP:
                        read_fill(h, 2 * j)
                    if j < STEPS:
                        maximum(h, j, 1)
                    for g in groups[:2]:
                        group_low(h, j - 1, g)
                    if j < GATE_STEP:
                        read_fill(h, 2 * j + 1)
                    for g in groups[2:]:
                        group_low(h, j - 1, g)
                dve.wait_ge(r_rms_made, h + 1)
                nc.vector.reciprocal(ro_rrms[:], ro_rms[:]).then_inc(r_rrms_made, 1)
                dve.wait_ge(r_rrms_made, h + 1)
                dve.wait_ge(r_gated, h + 1)
                out = ro[:].rearrange("p c (h n) -> p (c h) n", n=C)
                nc.vector.tensor_tensor(out, out, ro_rrms[:].unsqueeze(2).to_broadcast([P, CH * HEADS, C]), ALU.mult).then_inc(r_scaled, 1)
                dve.wait_ge(o_rms_made, h + 1)
                nc.vector.reciprocal(o_rrms[:], o_rms[:]).then_inc(o_rrms_made, 1)
                dve.wait_ge(o_rrms_made, h + 1)
                for j in range(STEPS):
                    nc.vector.tensor_scalar(o_all[:, j, :], o_all[:, j, :], o_rrms[:, j:j + 1], None, ALU.mult).then_inc(o_normed, 1)

        @block.tensor
        def _(pe):
            def score(h, j, m):
                q, b = slice(j % GROUP * P, (j % GROUP + 1) * P), j // GROUP % 2
                for r, (bank, key, width) in enumerate(runs[j, m]):
                    if freed[j, m, r]:
                        pe.wait_ge(exp_made, h * RUNS + freed[j, m, r])
                    for k in range(key, key + width, 512):
                        n = min(512, key + width - k)
                        at = bank * 512 + k - key
                        dst, keys = ring[:, at:at + n], k_hl[:, m, k:k + n]
                        diagonal = k + n == (j + 1) * P
                        pe.matmul(dst, q_hl[b][:, m, q], keys, start=True, stop=False)
                        if diagonal:
                            pe.matmul(ring[:, at + n - P:at + n], early[:], late[:], start=False, stop=False, skip_group_check=True)
                        last = pe.matmul(dst, q_lh[b][:, m, q], keys, start=False, stop=True)
                    last.then_inc(scored, 1)

            def turn(h, j, g):
                k = GROUP_AT[j, g]
                if g == 0:
                    pe.wait_ge(combined, h * STEPS + j + 1)
                if k >= 2:
                    pe.wait_ge(group_lo, h * GROUPS + k - 1)
                for t in range(tiles_in(j, g)):
                    key = (g * GROUP + t) * P
                    last = pe.transpose(turned[k % 2][:, t * P:(t + 1) * P], expo[j % 2][:, 0, key:key + P], ident[:])
                last.then_inc(group_turned, 1)

            def weigh(h, j, g):
                k = GROUP_AT[j, g]
                pe.wait_ge(group_lo, h * GROUPS + k + 1)
                if g == 0 and j:
                    pe.wait_ge(o_read, h * STEPS + j)
                for t in range(tiles_in(j, g)):
                    kt = g * GROUP + t
                    hi, lo = wt_hi[k % 2][:, t * P:(t + 1) * P], wt_lo[k % 2][:, t * P:(t + 1) * P]
                    pe.matmul(out_bank[:, 0:P], hi, v_hi[:, kt, :], start=kt == 0, stop=False)
                    pe.matmul(out_bank[:, 0:P], hi, v_lo[:, kt, :], start=False, stop=False)
                    last = pe.matmul(out_bank[:, 0:P], lo, v_hi[:, kt, :], start=False, stop=kt == j)
                last.then_inc(group_used, 1)

            def fill(h, n):
                kind, side, at = FILLS[n]
                fill_read.wait(pe, filled(h, n) - 1)
                if kind == "diagonal":
                    head = side * HALF + at
                    for c in range(CH):
                        tok = slice(c * C, (c + 1) * C)
                        last = pe.matmul(fill_bank[:, tok], rk[:, head, tok], rq[:, head, tok], start=True, stop=True)
                elif kind == "level":
                    pe.wait_ge(q_ready[side], h * UPDATES + at + 1)
                    if at:
                        pe.wait_ge(k_ready[side], h * LEVELS + at)
                    for hc in range(HC):
                        head, c = side * HALF + hc // CH, hc % CH
                        tok = slice(c * C, (c + 1) * C)
                        queries = rq[:, head, tok].rearrange("p (n s j) -> p n s j", s=2, j=1 << at)[:, :, 1, :]
                        dst = fill_bank[:, hc * RUN:(hc + 1) * RUN].rearrange("p (n j) -> p n j", j=1 << at)
                        last = pe.matmul(dst, rk[:, head, tok], queries, start=True, stop=True)
                elif kind == "k":
                    if at == 0:
                        for s in range(2):
                            pe.wait_ge(k_ready[s], h * LEVELS + LEVELS)
                    for head in range(HEADS):
                        last = pe.transpose(fill_bank[:, head * C:(head + 1) * C], rk[:, head, at * C:(at + 1) * C], ident[:])
                elif kind == "output":
                    if at == 0:
                        pe.wait_ge(rt_in, h * (16 * RT_DMAS) + 16 * RT_DMAS)
                        for s in range(2):
                            pe.wait_ge(q_ready[s], h * UPDATES + UPDATES)
                    for head in range(HEADS):
                        mine = slice(head * C, (head + 1) * C)
                        pe.matmul(fill_bank[:, mine], rscore[:, head, at], rv[:, at, mine], start=True, stop=False)
                        last = pe.matmul(fill_bank[:, mine], rq[:, head, at * C:(at + 1) * C], state[:, head, :], start=False, stop=True)
                else:
                    for head in range(HEADS):
                        mine = slice(head * C, (head + 1) * C)
                        last = pe.matmul(fill_bank[:, mine], k_tok[:, at, head, :], rv[:, at, mine], start=True, stop=True)
                last.then_inc(fill_done, 1)

            pe.wait_ge(masks_made, 4)
            with pe.Fori(0, HEADS) as h:
                pe.wait_ge(k_in[0], h * 32 + 32)
                for j in range(STEPS + 1):
                    groups = banks_of(j - 1) if j else 0
                    if j < STEPS:
                        if j % GROUP == 0:
                            pe.wait_ge(q_in[j // GROUP % 2], h * 128 + (j // GROUP // 2 + 1) * 64)
                        if j == GROUP:
                            pe.wait_ge(k_in[1], h * 32 + 32)
                        score(h, j, 0)
                    if j == 0:
                        pe.wait_ge(r_in, h * (16 * R_DMAS) + 16 * R_DMAS)
                    if j == 1:
                        pe.wait_ge(v_in[0], h * 32 + 32)
                    if j == GROUP + 1:
                        pe.wait_ge(v_in[1], h * 32 + 32)
                    if j < GATE_STEP:
                        fill(h, 2 * j)
                    for g in range(min(2, groups)):
                        turn(h, j - 1, g)
                    if j < STEPS:
                        score(h, j, 1)
                    if j < GATE_STEP:
                        fill(h, 2 * j + 1)
                    for g in range(groups):
                        weigh(h, j - 1, g)
                        if g + 2 < groups:
                            turn(h, j - 1, g + 2)
                for c in range(2 * TURNS):
                    if c < TURNS:
                        pe.wait_ge(o_normed, h * STEPS + (c + 1) * GROUP)
                    elif c == TURNS:
                        pe.wait_ge(r_scaled, h + 1)
                    if c >= 2:
                        pe.wait_ge(o_staged, h * (2 * TURNS) + c - 1)
                    for t in range(GROUP):
                        src = o_all[:, c * GROUP + t, :] if c < TURNS else ro[:, t, (c - TURNS) * C:(c - TURNS + 1) * C]
                        last = pe.transpose(turned[c % 2][:, t * P:(t + 1) * P], src, ident[:])
                    last.then_inc(o_turn_done, 1)


def feed(nc, x, mix, w_out, ffn_g, w_gate, w_up, w_down, ident, ones, eps, y):
    FS = D_FF // P
    OUTS = D // UC
    PAIRS = D_FF // UC
    CHUNKS = [range(s, min(s + KS, FS)) for s in range(0, FS, KS)]
    GATED = OUTS + 2 * PAIRS
    UNITS = GATED + OUTS * len(CHUNKS)
    assert UNITS % 2 == 0 and OUTS % 2 == 0

    with ExitStack() as ctx:
        a = Alloc(nc, ctx, "feed")
        g_col = a.sb("g_col", [P, KS])
        mix_raw = a.sb("mix_raw", [P, 2, TB])
        x_piece = a.sb("x_piece", [P, SUB, UC])
        x_mid = a.sb("x_mid", [P, KS, TB])
        h_hi = a.sb("h_hi", [P, KS, TB], F32R)
        h_lo = a.sb("h_lo", [P, KS, TB], F32R)
        w_raw = [a.sb(f"w_raw{b}", [P, KS, UC]) for b in range(2)]
        w_hi = [a.sb(f"w_hi{b}", [P, KS, UC], F32R) for b in range(2)]
        w_lo = [a.sb(f"w_lo{b}", [P, KS, UC], F32R) for b in range(2)]
        ff_hi = a.sb("ff_hi", [P, FS, TB], F32R)
        ff_lo = a.sb("ff_lo", [P, FS, TB], F32R)
        gate_work = a.sb("gate_work", [P, UT, TB])
        ff_work = a.sb("ff_work", [P, UT, TB])
        token_scale = a.sb("token_scale", [P, TB])
        rms = a.sb("rms", [P, SUB])
        rrms = a.sb("rrms", [P, SUB])
        wide = a.sb("wide", [P, SUB, P])
        prod = [[a.bank(f"prod{b}{t}") for t in range(UT)] for b in range(2)]
        turned = [a.bank(f"turned{t}") for t in range(UT)]
        sums = a.bank("sums")
        scales = a.bank("scales")

        waited = a.sem("waited")
        pe_waited = a.sem("pe_waited")
        gains_in = a.sem("gains_in")
        mix_in = [a.sem(f"mix_in{c}") for c in range(OUTS)]
        x_in = a.sem("x_in")
        w_in_sem = [a.sem(f"w_in{b}") for b in range(2)]
        w_hi_made = a.sem("w_hi_made")
        w_lo_made = a.sem("w_lo_made")
        unit_done = Count(a.sem("unit_done"), 1)
        mix_hi_made = a.sem("mix_hi_made")
        mix_lo_made = a.sem("mix_lo_made")
        x_mid_made = a.sem("x_mid_made")
        sq_made = a.sem("sq_made")
        sums_made = Count(a.sem("sums_made"), 1)
        rms_made = a.sem("rms_made")
        rrms_made = a.sem("rrms_made")
        widened = a.sem("widened")
        spread = a.sem("spread")
        token_scale_made = a.sem("token_scale_made")
        h_hi_made = a.sem("h_hi_made")
        h_lo_made = a.sem("h_lo_made")
        gate_scaled = a.sem("gate_scaled")
        sigmoid_made = a.sem("sigmoid_made")
        silu_made = a.sem("silu_made")
        gate_made = Count(a.sem("gate_made"), 1)
        ff_made = Count(a.sem("ff_made"), 1)
        ff_hi_made = a.sem("ff_hi_made")
        ff_lo_made = Count(a.sem("ff_lo_made"), 1)
        y_made = a.sem("y_made")
        y_turned = a.sem("y_turned")
        y_staged = a.sem("y_staged")
        y_stored = Count(a.sem("y_stored"), 16)
        block = ctx.enter_context(nc.Block())

        mix_view = mix.rearrange("(s p) n -> p s n", p=P)
        views = {"out": w_out.rearrange("(s p) n -> p s n", p=P), "gate": w_gate.rearrange("(s p) n -> p s n", p=P),
                 "up": w_up.rearrange("(s p) n -> p s n", p=P), "down": w_down.rearrange("(s p) n -> p s n", p=P)}

        def after(b):
            return ((b + 1) % BLOCKS) * TB

        def store_y(sp, b, c):
            sp.wait_ge(y_staged, b * (OUTS * UT) + (c + 1) * UT)
            sp.sem_inc(waited, 1)
            for t in range(UT):
                dst = y[bass.ds(b * TB, TB), c * UC + t * P:c * UC + (t + 1) * P].rearrange("(s p) n -> p s n", p=P)
                sp.dma_start(dst, ff_work[:, t, :].rearrange("p (s n) -> p s n", s=SUB)).then_inc(y_stored.sem, 16)

        def slabs_of(n):
            n = n % UNITS
            return KS if n < GATED else len(CHUNKS[(n - GATED) % len(CHUNKS)])

        def stage_y(act, b, c):
            y_stored.wait(act, b * (16 * UT * OUTS) + 16 * UT * c)
            for t in range(UT):
                act.wait_ge(y_turned, b * KS + c * UT + t + 1)
                nc.scalar.activation(ff_work[:, t, :], turned[t][:], ACT.Copy).then_inc(y_staged, 1)

        def mix_piece(c, first_block=False):
            if first_block and c >= 2:
                return x_mid[:, 2 * c:2 * c + 2, :]
            return (mix_raw, gate_work)[c % 2][:]

        @block.sync
        def _(sp):
            def load_w(n, kind, column, slabs=range(KS)):
                slot = n % 2
                sp.dma_start(w_raw[slot][:, 0:len(slabs), :],
                             views[kind][:, slabs[0]:slabs[-1] + 1, bass.ds(column, UC)]).then_inc(w_in_sem[slot], 16)

            def load_down(d):
                c, j = divmod(d, len(CHUNKS))
                load_w(d, "down", c * UC, CHUNKS[j])

            def split_done(b, n):
                sp.wait_ge(w_lo_made, b * UNITS + n + 1)

            def load_mix(tok, c, first_block=False):
                sp.dma_start(mix_piece(c, first_block), mix_view[:, 2 * c:2 * c + 2, bass.ds(tok, TB)]).then_inc(mix_in[c], 16)

            def load_x(tok, u):
                sp.dma_start(x_piece[:], x[bass.ds(tok, TB), u * UC:(u + 1) * UC].rearrange("(t p) n -> p t n", p=P)).then_inc(x_in, 16)

            load_w(0, "out", 0)
            for c in range(OUTS):
                load_mix(0, c, True)
            load_w(1, "out", UC)
            load_x(0, 0)
            sp.dma_start(g_col[:], ffn_g.rearrange("(s p) -> p s", p=P), allow_slow_non_contiguous=True).then_inc(gains_in, 16)
            with sp.Fori(0, BLOCKS) as b:
                for u in range(OUTS):
                    split_done(b, u)
                    if u + 2 < OUTS:
                        load_w(u, "out", (u + 2) * UC)
                    else:
                        load_w(u, ("gate", "up")[u + 2 - OUTS], 0)
                    if u + 1 < OUTS:
                        unit_done.wait(sp, b * UNITS + u + 1)
                        sp.sem_inc(waited, 1)
                        load_x(b * TB, u + 1)
                with sp.Fori(0, PAIRS - 1) as f:
                    for k, kind in enumerate(("gate", "up")):
                        sp.wait_ge(w_lo_made, b * UNITS + f * 2 + (OUTS + k + 1))
                        sp.sem_inc(waited, 1)
                        load_w(k, kind, f * UC + UC)
                for d in range(2):
                    split_done(b, GATED - 2 + d)
                    load_down(d)
                for d in range(OUTS * len(CHUNKS)):
                    c, j = divmod(d, len(CHUNKS))
                    split_done(b, GATED + d)
                    if d + 2 < OUTS * len(CHUNKS):
                        load_down(d + 2)
                    else:
                        load_w(d, "out", (d + 2 - OUTS * len(CHUNKS)) * UC)
                    if d == 0:
                        sp.wait_ge(mix_lo_made, b * OUTS + OUTS)
                        ff_made.wait(sp, b * FS + FS)
                        sp.sem_inc(waited, 1)
                        for piece in range(2):
                            load_mix(after(b), piece)
                        load_x(after(b), 0)
                    elif j == 0:
                        store_y(sp, b, c - 1)
                for piece in range(2, OUTS):
                    sp.wait_ge(mix_lo_made, b * OUTS + OUTS + piece - 1)
                    sp.sem_inc(waited, 1)
                    load_mix(after(b), piece)
                store_y(sp, b, OUTS - 1)
            y_stored.wait(sp, 16 * UT * OUTS * BLOCKS)
            sp.wait_ge(x_in, 16 * (OUTS * BLOCKS + 1))
            for c in range(OUTS):
                sp.wait_ge(mix_in[c], 16 * (BLOCKS + 1))
            for slot in range(2):
                sp.wait_ge(w_in_sem[slot], 16 * (UNITS // 2 * BLOCKS + 1))

        @block.scalar
        def _(act):
            def split_w(count, in_count, slot, slabs=KS):
                act.wait_ge(w_in_sem[slot], in_count)
                unit_done.wait(act, count - 1)
                nc.scalar.activation(w_hi[slot][:, 0:slabs, :], w_raw[slot][:, 0:slabs, :], ACT.Copy).then_inc(w_hi_made, 1)

            def split_unit(b, n):
                split_w(b * UNITS + n, b * (UNITS // 2 * 16) + 16 * (n // 2 + 1), n % 2, slabs_of(n))

            def split_mix(c, loads, first_block=False):
                act.wait_ge(mix_in[c], loads * 16)
                nc.scalar.activation(ff_hi[:, 2 * c:2 * c + 2, :], mix_piece(c, first_block), ACT.Copy).then_inc(mix_hi_made, 1)

            act.wait_ge(w_in_sem[0], 16)
            nc.scalar.activation(w_hi[0][:], w_raw[0][:], ACT.Copy).then_inc(w_hi_made, 1)
            for c in range(OUTS):
                split_mix(c, 1, True)
            act.wait_ge(gains_in, 16)
            with act.Fori(0, BLOCKS) as b:
                for u in range(OUTS):
                    split_unit(b, u + 1)
                    unit_done.wait(act, b * UNITS + u + 1)
                    for t in range(UT):
                        nc.scalar.activation(x_mid[:, u * UT + t, :], prod[u % 2][t][:], ACT.Copy).then_inc(x_mid_made, 1)
                    for t in range(UT):
                        s = u * UT + t
                        nc.scalar.activation(h_hi[:, s, :], prod[u % 2][t][:], ACT.Copy, scale=g_col[:, s:s + 1]).then_inc(h_hi_made, 1)
                    sums_made.wait(act, b * OUTS + u)
                    for t in range(UT):
                        act.wait_ge(x_mid_made, b * KS + u * UT + t + 1)
                        nc.scalar.activation(gate_work[:, t, :], x_mid[:, u * UT + t, :], ACT.Square).then_inc(sq_made, 1)
                split_unit(b, OUTS + 1)
                sums_made.wait(act, b * OUTS + OUTS)
                nc.scalar.activation(rms[:], sums[:, 0:SUB], ACT.Sqrt, bias=eps[:], scale=1.0 / D).then_inc(rms_made, 1)
                y_stored.wait(act, b * (16 * UT * OUTS))
                with act.Fori(0, PAIRS) as f:
                    for t in range(UT):
                        act.wait_ge(gate_scaled, b * FS + f * UT + (t + 1))
                        ff_lo_made.wait(act, b * FS + f * UT)
                        nc.scalar.activation(ff_work[:, t, :], gate_work[:, t, :], ACT.Sigmoid).then_inc(sigmoid_made, 1)
                    split_w(b * UNITS + f * 2 + (OUTS + 2), b * (UNITS // 2 * 16) + f * 16 + (OUTS // 2 + 2) * 16, 0)
                    for t in range(UT):
                        ff_made.wait(act, b * FS + f * UT + (t + 1))
                        nc.scalar.activation(ff_hi[:, bass.ds(f * UT + t, 1), :].rearrange("p o n -> p (o n)"),
                                             ff_work[:, t, :], ACT.Copy).then_inc(ff_hi_made, 1)
                    split_w(b * UNITS + f * 2 + (OUTS + 3), b * (UNITS // 2 * 16) + f * 16 + (OUTS // 2 + 2) * 16, 1)
                for d in range(OUTS * len(CHUNKS)):
                    c, j = divmod(d, len(CHUNKS))
                    if d:
                        split_unit(b, GATED + d + 1)
                    if c == OUTS - 1 and j:
                        for piece in range(2 * (j - 1), 2 * j):
                            split_mix(piece, b + 2)
                    if c and j == 1 or d == OUTS * len(CHUNKS) - 1:
                        stage_y(act, b, c - 1 if j == 1 else c)

        @block.vector
        def _(dve):
            def split_w(count, slot, slabs=KS):
                dve.wait_ge(w_hi_made, count + 1)
                nc.vector.tensor_tensor(w_lo[slot][:, 0:slabs, :], w_raw[slot][:, 0:slabs, :],
                                        w_hi[slot][:, 0:slabs, :].bitcast(F32), ALU.subtract).then_inc(w_lo_made, 1)

            def split_mix(c, count, first_block=False):
                dve.wait_ge(mix_hi_made, count)
                nc.vector.tensor_tensor(ff_lo[:, 2 * c:2 * c + 2, :], mix_piece(c, first_block), ff_hi[:, 2 * c:2 * c + 2, :].bitcast(F32),
                                        ALU.subtract).then_inc(mix_lo_made, 1)

            for count in (unit_done, gate_made, ff_made, ff_lo_made, sums_made, y_stored):
                dve.sem_inc(count.sem, count.credit)
            dve.wait_ge(w_hi_made, 1)
            nc.vector.tensor_tensor(w_lo[0][:], w_raw[0][:], w_hi[0][:].bitcast(F32), ALU.subtract).then_inc(w_lo_made, 1)
            for c in range(OUTS):
                split_mix(c, c + 1, True)
            dve.wait_ge(gains_in, 16)
            with dve.Fori(0, BLOCKS) as b:
                for u in range(OUTS):
                    split_w(b * UNITS + u + 1, (u + 1) % 2)
                    for t in range(UT):
                        s = u * UT + t
                        dve.wait_ge(h_hi_made, b * KS + s + 1)
                        nc.vector.scalar_tensor_tensor(out=h_lo[:, s, :], in0=x_mid[:, s, :], scalar=g_col[:, s:s + 1],
                                                       in1=h_hi[:, s, :].bitcast(F32), op0=ALU.mult, op1=ALU.subtract).then_inc(h_lo_made, 1)
                split_w(b * UNITS + (OUTS + 1), 1)
                dve.wait_ge(rms_made, b + 1)
                nc.vector.reciprocal(rrms[:], rms[:]).then_inc(rrms_made, 1)
                dve.wait_ge(rrms_made, b + 1)
                nc.vector.tensor_copy(wide[:], rrms[:].unsqueeze(2).to_broadcast([P, SUB, P])).then_inc(widened, 1)
                dve.wait_ge(spread, b + 1)
                gate_made.wait(dve, b * FS)
                nc.vector.tensor_copy(token_scale[:], scales[:]).then_inc(token_scale_made, 1)
                with dve.Fori(0, PAIRS) as f:
                    dve.wait_ge(token_scale_made, b + 1)
                    unit_done.wait(dve, b * UNITS + f * 2 + (OUTS + 1))
                    ff_made.wait(dve, b * FS + f * UT)
                    for t in range(UT):
                        nc.vector.tensor_tensor(gate_work[:, t, :], prod[0][t][:], token_scale[:], ALU.mult).then_inc(gate_scaled, 1)
                    for t in range(UT):
                        dve.wait_ge(sigmoid_made, b * FS + f * UT + (t + 1))
                        nc.vector.tensor_tensor(gate_work[:, t, :], gate_work[:, t, :], ff_work[:, t, :], ALU.mult).then_inc(silu_made, 1)
                    for t in range(UT):
                        dve.wait_ge(silu_made, b * FS + f * UT + (t + 1))
                        nc.vector.tensor_tensor(gate_work[:, t, :], gate_work[:, t, :], token_scale[:], ALU.mult).then_inc(gate_made.sem, 1)
                    split_w(b * UNITS + f * 2 + (OUTS + 2), 0)
                    unit_done.wait(dve, b * UNITS + f * 2 + (OUTS + 2))
                    for t in range(UT):
                        gate_made.wait(dve, b * FS + f * UT + (t + 1))
                        nc.vector.tensor_tensor(ff_work[:, t, :], prod[1][t][:], gate_work[:, t, :], ALU.mult).then_inc(ff_made.sem, 1)
                    for t in range(UT):
                        slab = bass.ds(f * UT + t, 1)
                        dve.wait_ge(ff_hi_made, b * FS + f * UT + (t + 1))
                        nc.vector.tensor_tensor(ff_lo[:, slab, :].rearrange("p o n -> p (o n)"), ff_work[:, t, :],
                                                ff_hi[:, slab, :].rearrange("p o n -> p (o n)").bitcast(F32),
                                                ALU.subtract).then_inc(ff_lo_made.sem, 1)
                    split_w(b * UNITS + f * 2 + (OUTS + 3), 1)
                for d in range(OUTS * len(CHUNKS)):
                    c, j = divmod(d, len(CHUNKS))
                    if d:
                        split_w(b * UNITS + GATED + d + 1, (d + 1) % 2, slabs_of(GATED + d + 1))
                    if c == OUTS - 1 and j:
                        for piece in range(2 * (j - 1), 2 * j):
                            split_mix(piece, b * OUTS + OUTS + piece + 1)
                    if j == len(CHUNKS) - 1:
                        unit_done.wait(dve, b * UNITS + GATED + d + 1)
                        for t in range(UT):
                            s = c * UT + t
                            nc.vector.tensor_tensor(x_mid[:, s, :], prod[c % 2][t][:], x_mid[:, s, :], ALU.add).then_inc(y_made, 1)

        @block.tensor
        def _(pe):
            def slab_product(dst, slot, col, k, s, hi, lo, first, stop):
                pe.matmul(dst, w_hi[slot][:, k, col], hi[:, s, :], start=first, stop=False)
                pe.matmul(dst, w_hi[slot][:, k, col], lo[:, s, :], start=False, stop=False)
                return pe.matmul(dst, w_lo[slot][:, k, col], hi[:, s, :], start=False, stop=stop)

            def product(dst, slot, col, slabs, hi, lo, first, stop):
                for k, s in enumerate(slabs):
                    last = slab_product(dst, slot, col, k, s, hi, lo, first and k == 0, stop and k == len(slabs) - 1)
                return last

            def sum_squares(b, u):
                for t in range(UT):
                    pe.wait_ge(sq_made, b * KS + u * UT + t + 1)
                    for r in range(SUB):
                        last = pe.matmul(sums[:, r:r + 1], gate_work[:, t, r * P:(r + 1) * P], ones[:, 0:1],
                                         start=u == 0 and t == 0 and r == 0, stop=u == OUTS - 1 and t == UT - 1,
                                         skip_group_check=True)
                last.then_inc(sums_made.sem, 1)

            def turn_y(b, c):
                for t in range(UT):
                    s = c * UT + t
                    pe.wait_ge(y_made, b * KS + s + 1)
                    if c:
                        pe.wait_ge(y_staged, b * KS + s - UT + 1)
                    for r in range(SUB):
                        last = pe.transpose(turned[t][:, r * P:(r + 1) * P], x_mid[:, s, r * P:(r + 1) * P], ident[:])
                    last.then_inc(y_turned, 1)

            def up_unit(b, f):
                pe.wait_ge(w_lo_made, b * UNITS + f * 2 + (OUTS + 2))
                ff_made.wait(pe, b * FS + f * UT)
                for t in range(UT):
                    last = product(prod[1][t][:], 1, slice(t * P, (t + 1) * P), range(KS), h_hi, h_lo, True, True)
                last.then_inc(unit_done.sem, 1)

            with pe.Fori(0, BLOCKS) as b:
                for u in range(OUTS):
                    pe.wait_ge(w_lo_made, b * UNITS + u + 1)
                    if u >= 2:
                        pe.wait_ge(h_hi_made, b * KS + (u - 1) * UT)
                    for t in range(UT):
                        col = slice(t * P, (t + 1) * P)
                        if u == 0 and t == 0:
                            for s in range(0, KS, 2):
                                pe.wait_ge(mix_lo_made, b * OUTS + s // 2 + 1)
                                for k in range(s, s + 2):
                                    slab_product(prod[0][t][:], 0, col, k, k, ff_hi, ff_lo, k == 0, False)
                        else:
                            product(prod[u % 2][t][:], u % 2, col, range(KS), ff_hi, ff_lo, True, False)
                        if t == 0:
                            pe.wait_ge(x_in, b * (16 * OUTS) + 16 * (u + 1))
                            if u:
                                sum_squares(b, u - 1)
                        for r in range(SUB):
                            last = pe.matmul(prod[u % 2][t][:, r * P:(r + 1) * P], x_piece[:, r, col], ident[:],
                                             start=False, stop=r == SUB - 1)
                    last.then_inc(unit_done.sem, 1)
                pe.wait_ge(w_lo_made, b * UNITS + OUTS + 1)
                for s in range(KS):
                    pe.wait_ge(h_lo_made, b * KS + s + 1)
                    for t in range(UT):
                        last = slab_product(prod[0][t][:], 0, slice(t * P, (t + 1) * P), s, s, h_hi, h_lo, s == 0, s == KS - 1)
                    if s == KS // 2:
                        sum_squares(b, OUTS - 1)
                last.then_inc(unit_done.sem, 1)
                pe.wait_ge(widened, b + 1)
                for r in range(SUB):
                    last = pe.matmul(scales[:, r * P:(r + 1) * P], wide[:, r, :], ident[:], start=True, stop=True)
                last.then_inc(spread, 1)
                with pe.Fori(0, PAIRS - 1) as f:
                    up_unit(b, f)
                    pe.wait_ge(w_lo_made, b * UNITS + f * 2 + (OUTS + 3))
                    pe.wait_ge(gate_scaled, b * FS + f * UT + UT)
                    for t in range(UT):
                        last = product(prod[0][t][:], 0, slice(t * P, (t + 1) * P), range(KS), h_hi, h_lo, True, True)
                    last.then_inc(unit_done.sem, 1)
                up_unit(b, PAIRS - 1)
                for d in range(OUTS * len(CHUNKS)):
                    c, j = divmod(d, len(CHUNKS))
                    n, slabs = GATED + d, CHUNKS[j]
                    pe.wait_ge(w_lo_made, b * UNITS + n + 1)
                    if d == 0:
                        pe.wait_ge(gate_scaled, b * FS + FS)
                    if c == 0:
                        ff_lo_made.wait(pe, b * FS + slabs[-1] + 1)
                    for t in range(UT):
                        last = product(prod[c % 2][t][:], n % 2, slice(t * P, (t + 1) * P), slabs, ff_hi, ff_lo,
                                       j == 0, j == len(CHUNKS) - 1)
                        if c and j == 0 and t == 0:
                            turn_y(b, c - 1)
                    last.then_inc(unit_done.sem, 1)
                turn_y(b, OUTS - 1)


def hybrid_trunk_kernel(nc, x, attn_norm_g, w_in, q_norm_g, k_norm_g, lambda_q1, lambda_k1, lambda_q2, lambda_k2,
                        subln_g, lower_bounds, hgrn_norm_g, w_out, ffn_norm_g, w_gate, w_up, w_down, out):
    def scratch(name, shape):
        return nc.dram_tensor(name, shape, F32).ap()

    mid = {
        "qk_hi": scratch("qk_hi", (2 * W, SEQ)), "qk_lo": scratch("qk_lo", (2 * W, SEQ)),
        "v_hi": scratch("v_hi", (SEQ, W)), "v_lo": scratch("v_lo", (SEQ, W)),
        "hq": scratch("hq", (W, SEQ)), "hf": scratch("hf", (W, SEQ)), "hk": scratch("hk", (W, SEQ)),
        "hv": scratch("hv", (SEQ, W)), "hgate": scratch("hgate", (SEQ, W)),
    }
    mix = scratch("mix", (D, SEQ))
    with ExitStack() as ctx:
        a = Alloc(nc, ctx, "all")
        ident, ones = (a.sb(n, [P, P]) for n in ("ident", "ones"))
        pair_sel = a.sb("pair_sel", [P, 2])
        eps = a.sb("eps", [P, 1])
        make_constants(nc, ident, pair_sel, ones, eps)
        with ExitStack() as both:
            masks = Alloc(nc, both, "level").sb("masks", [P, HGRN_LEVELS, HEADS // 2 * TB // 2], mybir.dt.uint8)
            project(nc, x[0], attn_norm_g[0], w_in[0], q_norm_g[0], k_norm_g[0], ident, pair_sel, eps, mid, masks)
            mix_tokens(nc, mid, (lambda_q1[0], lambda_k1[0], lambda_q2[0], lambda_k2[0]), subln_g[0], hgrn_norm_g[0],
                       ident, eps, masks, mix)
        feed(nc, x[0], mix, w_out[0], ffn_norm_g[0], w_gate[0], w_up[0], w_down[0], ident, ones, eps, out[0])


_INS = ['x', 'attn_norm_g', 'w_in', 'q_norm_g', 'k_norm_g', 'lambda_q1', 'lambda_k1', 'lambda_q2', 'lambda_k2',
        'subln_g', 'lower_bounds', 'hgrn_norm_g', 'w_out', 'ffn_norm_g', 'w_gate', 'w_up', 'w_down']
_OUTS = [((1, 2048, 1024), 'float32')]


def kernel(**inputs):
    import numpy as _np
    import concourse.bacc as _bacc
    from concourse import mybir as _mybir
    from concourse.bass_utils import run_bass_kernel_spmd as _run

    nc = _bacc.Bacc("TRN2", target_bir_lowering=False, num_devices=1)
    arrays, args = {}, []
    for name in _INS:
        a = _np.ascontiguousarray(inputs[name])
        arrays[f"in_{name}_dram"] = a
        args.append(nc.dram_tensor(f"in_{name}_dram", a.shape, _mybir.dt.from_np(a.dtype), kind="ExternalInput").ap())
    for i, (shape, dtype) in enumerate(_OUTS):
        dt = _mybir.dt.from_np(_np.dtype(dtype))
        args.append(nc.dram_tensor(f"out_{i}_dram", shape, dt, kind="ExternalOutput").ap())
    hybrid_trunk_kernel(nc, *args)
    r = _run(nc, [arrays], core_ids=[0])
    got = tuple(r.results[0][f"out_{i}_dram"] for i in range(len(_OUTS)))
    return got[0]
```
